# Optimizing a Trainium2 kernel written in Bass

```python
import numpy as np
import jax
import jax.numpy as jnp
from jax import lax

D_MODEL = 1024
BATCH = 1
SEQ = 256
DEPTH = 2

HEAD_DIM = 64
N_HEADS_MIX = 4
MIX_WIDTH = N_HEADS_MIX * HEAD_DIM
N_BRANCH = 4
ROPE_THETA = 10000.0
NORM_EPS = 1e-6
Q_BLOCK = 128
GATHER_QBLOCK = 64
NEG_INF = -1e30

NSA_CMP_LEN = 32
NSA_CMP_STRIDE = 16
NSA_CMP_HIDDEN = 256
NSA_SEL_BLOCK = 64
NSA_N_SEL = 16
NSA_WINDOW = 512
NSA_N_GATES = 3
NSA_FORCE_SCORE = 1e4

FOX_BIAS_INIT = 3.0

DSA_KV_RANK = 128
DSA_IDX_HEADS = 4
DSA_IDX_DIM = 64
DSA_TOPK_MAX = 256

SWA_WINDOW = 128
SWA_KV_HEADS = 2

MOE_GROUPS = 8
MOE_EXPERTS_PER_GROUP = 8
MOE_N_EXPERTS = MOE_GROUPS * MOE_EXPERTS_PER_GROUP
MOE_TOPK = 2
MOE_D_EXPERT = 256
MOE_ROW_BLOCK = 256

IN_SPLITS = (
    ('q_a', MIX_WIDTH), ('k_cmp', HEAD_DIM), ('v_cmp', HEAD_DIM),
    ('k_sel', HEAD_DIM), ('v_sel', HEAD_DIM), ('k_win', HEAD_DIM), ('v_win', HEAD_DIM),
    ('g_a', N_HEADS_MIX * NSA_N_GATES),
    ('q_b', MIX_WIDTH), ('k_b', MIX_WIDTH), ('v_b', MIX_WIDTH), ('f_b', N_HEADS_MIX),
    ('q_c', MIX_WIDTH), ('ckv_c', DSA_KV_RANK), ('qi_c', DSA_IDX_HEADS * DSA_IDX_DIM),
    ('ki_c', DSA_IDX_DIM), ('wi_c', DSA_IDX_HEADS),
    ('q_d', MIX_WIDTH), ('k_d', SWA_KV_HEADS * HEAD_DIM), ('v_d', SWA_KV_HEADS * HEAD_DIM),
)
D_IN = sum(w for _, w in IN_SPLITS)

kernel_name = 'hybrid_nsa_fox_dsa_swa_hmoe'

def rms_norm(x, gain):
    xf = x.astype(jnp.float32)
    y = xf * lax.rsqrt(jnp.mean(xf * xf, axis=-1, keepdims=True) + NORM_EPS)
    return (y * gain.astype(jnp.float32)).astype(x.dtype)

def rope(x, positions):
    half = x.shape[-1] // 2
    inv_freq = ROPE_THETA ** (-jnp.arange(half, dtype=jnp.float32) / half)
    ang = positions.astype(jnp.float32)[..., None] * inv_freq
    cos = jnp.cos(ang)[:, :, None, :]
    sin = jnp.sin(ang)[:, :, None, :]
    xf = x.astype(jnp.float32)
    x1, x2 = xf[..., :half], xf[..., half:]
    return jnp.concatenate([x1 * cos - x2 * sin, x2 * cos + x1 * sin], axis=-1).astype(x.dtype)

def masked_softmax(logits, mask):
    p = jax.nn.softmax(jnp.where(mask, logits, NEG_INF), axis=-1)
    return jnp.where(mask, p, 0.0)

def split_in(z):
    out = {}
    off = 0
    for name, width in IN_SPLITS:
        out[name] = z[..., off:off + width]
        off += width
    return out

def banded_attention(q, k, v, window, sinks=None):
    B, S, H, dh = q.shape
    KV = k.shape[2]
    G = H // KV
    nb, nw = S // Q_BLOCK, window // Q_BLOCK
    pad = ((0, 0), (window, 0), (0, 0), (0, 0))
    kp = jnp.pad(k, pad).reshape(B, nb + nw, Q_BLOCK, KV, dh)
    vp = jnp.pad(v, pad).reshape(B, nb + nw, Q_BLOCK, KV, dh)
    k_band = jnp.concatenate([kp[:, j:j + nb] for j in range(nw + 1)], axis=2)
    v_band = jnp.concatenate([vp[:, j:j + nb] for j in range(nw + 1)], axis=2)
    s_all = np.arange(-window, S).reshape(nb + nw, Q_BLOCK)
    s_band = np.concatenate([s_all[j:j + nb] for j in range(nw + 1)], axis=1)
    t_blk = np.arange(S).reshape(nb, Q_BLOCK)
    rel = t_blk[:, :, None] - s_band[:, None, :]
    mask = (rel >= 0) & (rel < window) & (s_band[:, None, :] >= 0)
    qb = q.reshape(B, nb, Q_BLOCK, KV, G, dh)
    s = jnp.einsum('bnqhgd,bnshd->bnhgqs', qb, k_band).astype(jnp.float32) * dh ** -0.5
    s = jnp.where(mask[None, :, None, None], s, NEG_INF)
    if sinks is not None:
        sink = jnp.broadcast_to(sinks.astype(jnp.float32).reshape(1, 1, KV, G, 1, 1), s.shape[:-1] + (1,))
        p = jax.nn.softmax(jnp.concatenate([s, sink], axis=-1), axis=-1)[..., :-1]
    else:
        p = jax.nn.softmax(s, axis=-1)
    o = jnp.einsum('bnhgqs,bnshd->bnqhgd', p.astype(v.dtype), v_band)
    return o.reshape(B, S, H, dh)

def nsa_compress(blocks, pe, w1, w2):
    B, n, L, dh = blocks.shape
    z = (blocks + pe).reshape(B, n, L * dh)
    return jax.nn.gelu(z @ w1) @ w2

def nsa_mixer(q, k_cmp, v_cmp, k_sel, v_sel, k_win, v_win, gate_logits, pe_k, w1_k, w2_k, pe_v, w1_v, w2_v):
    B, S, H, dh = q.shape
    scale = dh ** -0.5
    t = np.arange(S)
    n_cmp = (S - NSA_CMP_LEN) // NSA_CMP_STRIDE + 1
    win = np.arange(n_cmp)[:, None] * NSA_CMP_STRIDE + np.arange(NSA_CMP_LEN)[None, :]
    kc = nsa_compress(k_cmp[:, win], pe_k, w1_k, w2_k)
    vc = nsa_compress(v_cmp[:, win], pe_v, w1_v, w2_v)
    mask_c = win[:, -1][None, :] <= t[:, None]
    s_c = jnp.einsum('bthd,bcd->bhtc', q, kc).astype(jnp.float32) * scale
    p_c = masked_softmax(s_c, mask_c)
    o_cmp = jnp.einsum('bhtc,bcd->bthd', p_c.astype(vc.dtype), vc)
    n_blk = S // NSA_SEL_BLOCK
    c0 = np.arange(n_cmp) * NSA_CMP_STRIDE
    b0 = np.arange(n_blk) * NSA_SEL_BLOCK
    overlap = ((c0[:, None] < b0[None, :] + NSA_SEL_BLOCK) & (c0[:, None] + NSA_CMP_LEN > b0[None, :])).astype(np.float32)
    imp = jnp.einsum('bhtc,cj->btj', p_c, jnp.asarray(overlap))
    cur = (t // NSA_SEL_BLOCK)[:, None]
    j = np.arange(n_blk)[None, :]
    forced = (j == 0) | (j == cur) | (j == cur - 1)
    imp = jnp.where(forced, NSA_FORCE_SCORE, imp)
    imp = jnp.where(j > cur, -NSA_FORCE_SCORE, imp)
    n_sel = min(NSA_N_SEL, n_blk)
    _, sel = lax.top_k(imp, n_sel)
    kb = k_sel.reshape(B, n_blk, NSA_SEL_BLOCK, dh)
    vb = v_sel.reshape(B, n_blk, NSA_SEL_BLOCK, dh)
    ng = S // GATHER_QBLOCK
    q_g = q.reshape(B, ng, GATHER_QBLOCK, H, dh).swapaxes(0, 1)
    sel_g = sel.reshape(B, ng, GATHER_QBLOCK, n_sel).swapaxes(0, 1)
    t_g = jnp.arange(S).reshape(ng, GATHER_QBLOCK)
    offs = jnp.arange(NSA_SEL_BLOCK)
    take = jax.vmap(lambda tbl, idx: tbl[idx])
    n_keys = n_sel * NSA_SEL_BLOCK

    def sel_block(args):
        q_i, idx_i, t_i = args
        k_i = take(kb, idx_i).reshape(B, GATHER_QBLOCK, n_keys, dh)
        v_i = take(vb, idx_i).reshape(B, GATHER_QBLOCK, n_keys, dh)
        pos = (idx_i[..., None] * NSA_SEL_BLOCK + offs).reshape(B, GATHER_QBLOCK, n_keys)
        valid = pos <= t_i[None, :, None]
        s = jnp.einsum('bqhd,bqkd->bhqk', q_i, k_i).astype(jnp.float32) * scale
        p = masked_softmax(s, valid[:, None])
        return jnp.einsum('bhqk,bqkd->bqhd', p.astype(v_i.dtype), v_i)

    o_sel = lax.map(sel_block, (q_g, sel_g, t_g)).swapaxes(0, 1).reshape(B, S, H, dh)
    o_win = banded_attention(q, k_win[:, :, None, :], v_win[:, :, None, :], NSA_WINDOW)
    g = jax.nn.sigmoid(gate_logits.astype(jnp.float32)).astype(q.dtype)
    return g[..., 0:1] * o_cmp + g[..., 1:2] * o_sel + g[..., 2:3] * o_win

def fox_mixer(q, k, v, f_logit, f_bias):
    B, S, H, dh = q.shape
    scale = dh ** -0.5
    logf = jax.nn.log_sigmoid(f_logit.astype(jnp.float32) + f_bias.astype(jnp.float32))
    cum = jnp.cumsum(logf, axis=1).swapaxes(1, 2)
    nb = S // Q_BLOCK
    q_b = q.reshape(B, nb, Q_BLOCK, H, dh).swapaxes(0, 1)
    c_b = cum.reshape(B, H, nb, Q_BLOCK).transpose(2, 0, 1, 3)
    t_b = jnp.arange(S).reshape(nb, Q_BLOCK)
    key_pos = jnp.arange(S)

    def blk(args):
        q_i, c_i, t_i = args
        s = jnp.einsum('bqhd,bshd->bhqs', q_i, k).astype(jnp.float32) * scale
        s = s + (c_i[..., None] - cum[:, :, None, :])
        p = masked_softmax(s, key_pos[None, :] <= t_i[:, None])
        return jnp.einsum('bhqs,bshd->bqhd', p.astype(v.dtype), v)

    return lax.map(blk, (q_b, c_b, t_b)).swapaxes(0, 1).reshape(B, S, H, dh)

def dsa_mixer(q, k, v, q_idx, k_idx, w_idx):
    B, S, H, dh = q.shape
    n_ih, d_i = q_idx.shape[2], q_idx.shape[3]
    scale = dh ** -0.5
    top_k = min(DSA_TOPK_MAX, S // 4)
    ng = S // GATHER_QBLOCK
    w = w_idx.astype(jnp.float32) * n_ih ** -0.5
    q_g = q.reshape(B, ng, GATHER_QBLOCK, H, dh).swapaxes(0, 1)
    qi_g = q_idx.reshape(B, ng, GATHER_QBLOCK, n_ih, d_i).swapaxes(0, 1)
    w_g = w.reshape(B, ng, GATHER_QBLOCK, n_ih).swapaxes(0, 1)
    t_g = jnp.arange(S).reshape(ng, GATHER_QBLOCK)
    key_pos = jnp.arange(S)
    take = jax.vmap(lambda tbl, idx: tbl[idx])

    def blk(args):
        q_i, qi_i, w_i, t_i = args
        logit = jnp.einsum('bqhd,bsd->bqhs', qi_i, k_idx).astype(jnp.float32) * d_i ** -0.5
        score = jnp.einsum('bqh,bqhs->bqs', w_i, jax.nn.relu(logit))
        score = jnp.where(key_pos[None, None, :] <= t_i[None, :, None], score, NEG_INF)
        _, idx = lax.top_k(score, top_k)
        valid = idx <= t_i[None, :, None]
        k_i = take(k, idx)
        v_i = take(v, idx)
        s = jnp.einsum('bqhd,bqkhd->bhqk', q_i, k_i).astype(jnp.float32) * scale
        p = masked_softmax(s, valid[:, None])
        return jnp.einsum('bhqk,bqkhd->bqhd', p.astype(v_i.dtype), v_i)

    return lax.map(blk, (q_g, qi_g, w_g, t_g)).swapaxes(0, 1).reshape(B, S, H, dh)

def hier_moe(x, w_group, b_group, w_expert, b_expert, w_gate, w_up, w_down):
    B, S, D = x.shape
    T = B * S
    N = T * MOE_TOPK
    xf = x.reshape(T, D)
    g_logits = (xf @ w_group).astype(jnp.float32) + b_group.astype(jnp.float32)
    grp = jnp.argmax(g_logits, axis=-1)
    p_grp = jnp.take_along_axis(jax.nn.softmax(g_logits, axis=-1), grp[:, None], axis=1)[:, 0]
    e_logits = ((xf @ w_expert).astype(jnp.float32) + b_expert.astype(jnp.float32)).reshape(T, MOE_GROUPS, MOE_EXPERTS_PER_GROUP)
    e_in_grp = jnp.take_along_axis(e_logits, grp[:, None, None], axis=1)[:, 0]
    top_val, top_loc = lax.top_k(e_in_grp, MOE_TOPK)
    weights = (p_grp[:, None] * jax.nn.softmax(top_val, axis=-1)).reshape(N)
    expert_id = (grp[:, None] * MOE_EXPERTS_PER_GROUP + top_loc).reshape(N)
    token_id = jnp.repeat(jnp.arange(T, dtype=jnp.int32), MOE_TOPK)
    order = jnp.argsort(expert_id)
    e_sorted = expert_id[order]
    counts = jnp.bincount(expert_id, length=MOE_N_EXPERTS)
    padded = (counts + MOE_ROW_BLOCK - 1) // MOE_ROW_BLOCK * MOE_ROW_BLOCK
    start = jnp.cumsum(counts) - counts
    p_end = jnp.cumsum(padded)
    p_start = p_end - padded
    dest = p_start[e_sorted] + jnp.arange(N) - start[e_sorted]
    n_blocks = -(-(N + MOE_N_EXPERTS * (MOE_ROW_BLOCK - 1)) // MOE_ROW_BLOCK)
    rows = n_blocks * MOE_ROW_BLOCK
    row_tok = jnp.zeros((rows,), jnp.int32).at[dest].set(token_id[order])
    row_w = jnp.zeros((rows,), jnp.float32).at[dest].set(weights[order])
    blk_expert = jnp.minimum(jnp.searchsorted(p_end, jnp.arange(n_blocks) * MOE_ROW_BLOCK, side='right'), MOE_N_EXPERTS - 1)

    def expert_block(args):
        tok, e = args
        xt = xf[tok]
        return (jax.nn.silu(xt @ w_gate[e]) * (xt @ w_up[e])) @ w_down[e]

    y = lax.map(expert_block, (row_tok.reshape(n_blocks, MOE_ROW_BLOCK), blk_expert)).reshape(rows, D)
    out = jnp.zeros((T, D), x.dtype).at[row_tok].add(y * row_w[:, None].astype(y.dtype))
    return out.reshape(B, S, D)

def setup_inputs(seed: int = 0) -> dict:
    key = jax.random.key(seed)
    ks = iter(jax.random.split(key, 40))
    nrm = lambda shape, scale: jax.random.normal(next(ks), shape, jnp.float32) * scale
    L, D, dh, W = DEPTH, D_MODEL, HEAD_DIM, MIX_WIDTH
    E, DE = MOE_N_EXPERTS, MOE_D_EXPERT
    return {
        'x': nrm((BATCH, SEQ, D), 1.0),
        'positions': jnp.broadcast_to(jnp.arange(SEQ, dtype=jnp.int32), (BATCH, SEQ)),
        'attn_norm': 1.0 + nrm((L, D), 0.02),
        'w_in': nrm((L, D, D_IN), D ** -0.5),
        'nsa_pe_k': nrm((L, NSA_CMP_LEN, dh), 0.02),
        'nsa_w1_k': nrm((L, NSA_CMP_LEN * dh, NSA_CMP_HIDDEN), (NSA_CMP_LEN * dh) ** -0.5),
        'nsa_w2_k': nrm((L, NSA_CMP_HIDDEN, dh), NSA_CMP_HIDDEN ** -0.5),
        'nsa_pe_v': nrm((L, NSA_CMP_LEN, dh), 0.02),
        'nsa_w1_v': nrm((L, NSA_CMP_LEN * dh, NSA_CMP_HIDDEN), (NSA_CMP_LEN * dh) ** -0.5),
        'nsa_w2_v': nrm((L, NSA_CMP_HIDDEN, dh), NSA_CMP_HIDDEN ** -0.5),
        'fox_forget_bias': FOX_BIAS_INIT + nrm((L, N_HEADS_MIX), 0.1),
        'dsa_kv_norm': 1.0 + nrm((L, DSA_KV_RANK), 0.02),
        'dsa_w_ukv': nrm((L, DSA_KV_RANK, 2 * W), DSA_KV_RANK ** -0.5),
        'swa_sinks': nrm((L, N_HEADS_MIX), 0.5),
        'w_branch': nrm((L, N_BRANCH, W, D), W ** -0.5),
        'w_gate': nrm((L, N_BRANCH, D, D), D ** -0.5),
        'w_out': nrm((L, D, D), D ** -0.5),
        'ffn_norm': 1.0 + nrm((L, D), 0.02),
        'moe_w_group': nrm((L, D, MOE_GROUPS), D ** -0.5),
        'moe_b_group': nrm((L, MOE_GROUPS), 0.01),
        'moe_w_expert': nrm((L, D, E), D ** -0.5),
        'moe_b_expert': nrm((L, E), 0.01),
        'moe_w_gate': nrm((L, E, D, DE), D ** -0.5),
        'moe_w_up': nrm((L, E, D, DE), D ** -0.5),
        'moe_w_down': nrm((L, E, DE, D), DE ** -0.5),
        'final_norm': 1.0 + nrm((D,), 0.02),
    }

def reference(x, positions, attn_norm, w_in, nsa_pe_k, nsa_w1_k, nsa_w2_k, nsa_pe_v, nsa_w1_v, nsa_w2_v,
              fox_forget_bias, dsa_kv_norm, dsa_w_ukv, swa_sinks, w_branch, w_gate, w_out, ffn_norm,
              moe_w_group, moe_b_group, moe_w_expert, moe_b_expert, moe_w_gate, moe_w_up, moe_w_down,
              final_norm):
    B, S, D = x.shape
    H = N_HEADS_MIX
    heads = lambda a, n: a.reshape(B, S, n, HEAD_DIM)
    rope1 = lambda a: rope(a[:, :, None, :], positions)[:, :, 0, :]
    h = x
    for l in range(DEPTH):
        hn = rms_norm(h, attn_norm[l])
        z = split_in(hn @ w_in[l])
        o_a = nsa_mixer(
            rope(heads(z['q_a'], H), positions),
            rope1(z['k_cmp']), z['v_cmp'], rope1(z['k_sel']), z['v_sel'], rope1(z['k_win']), z['v_win'],
            z['g_a'].reshape(B, S, H, NSA_N_GATES),
            nsa_pe_k[l], nsa_w1_k[l], nsa_w2_k[l], nsa_pe_v[l], nsa_w1_v[l], nsa_w2_v[l])
        o_b = fox_mixer(heads(z['q_b'], H), heads(z['k_b'], H), heads(z['v_b'], H), z['f_b'], fox_forget_bias[l])
        kv_c = rms_norm(z['ckv_c'], dsa_kv_norm[l]) @ dsa_w_ukv[l]
        o_c = dsa_mixer(
            rope(heads(z['q_c'], H), positions),
            rope(heads(kv_c[..., :MIX_WIDTH], H), positions),
            heads(kv_c[..., MIX_WIDTH:], H),
            rope(z['qi_c'].reshape(B, S, DSA_IDX_HEADS, DSA_IDX_DIM), positions),
            rope1(z['ki_c']), z['wi_c'])
        o_d = banded_attention(
            rope(heads(z['q_d'], H), positions),
            rope(heads(z['k_d'], SWA_KV_HEADS), positions),
            heads(z['v_d'], SWA_KV_HEADS), SWA_WINDOW, swa_sinks[l])
        merged = jnp.zeros_like(h)
        for i, o in enumerate((o_a, o_b, o_c, o_d)):
            gate = jax.nn.sigmoid((hn @ w_gate[l, i]).astype(jnp.float32)).astype(h.dtype)
            merged = merged + gate * (o.reshape(B, S, MIX_WIDTH) @ w_branch[l, i])
        h = h + merged @ w_out[l]
        h = h + hier_moe(rms_norm(h, ffn_norm[l]), moe_w_group[l], moe_b_group[l], moe_w_expert[l],
                         moe_b_expert[l], moe_w_gate[l], moe_w_up[l], moe_w_down[l])
    return rms_norm(h, final_norm)


_drawn_inputs = setup_inputs


def setup_inputs(seed=0):
    import zlib

    import numpy as np

    out = dict(_drawn_inputs(seed))
    spreads = {}
    factors = {'nsa_pe_k': 29.16,
     'nsa_pe_v': 3.504,
     'dsa_kv_norm': 4.414,
     'swa_sinks': 4.602,
     'moe_b_group': 4.956,
     'moe_b_expert': 3.112,
     'final_norm': 8.152}
    for name, (base, spread) in spreads.items():
        noise = np.random.default_rng([zlib.crc32(name.encode()), seed]).standard_normal(out[name].shape)
        drawn = base * np.exp(spread * noise) if base else spread * noise
        out[name] = jnp.asarray(drawn.astype(out[name].dtype))
    for name, factor in factors.items():
        out[name] = (out[name] * factor).astype(out[name].dtype)
    return out
```

```python
from contextlib import ExitStack

import numpy as np

import concourse.bass as bass
from concourse import mybir

F32 = mybir.dt.float32
F32R = mybir.dt.float32r
I32 = mybir.dt.int32
ALU = mybir.AluOpType
ACT = mybir.ActivationFunctionType
AXX = mybir.AxisListType.X

P = 128
D = 1024
T = 256
NT = T // P
KC = D // P
DEPTH = 2
DH = 64
H = 4
W = H * DH
CMP_LEN, CMP_STRIDE, CMP_HID = 32, 16, 256
N_CMP = (T - CMP_LEN) // CMP_STRIDE + 1
TOPK = T // 4
SWA_WIN = 128
GROUPS, PER_GROUP = 8, 8
E = GROUPS * PER_GROUP
DE = 256
PAIRS = 2 * T
BLK = 128
NBLK = E + (PAIRS - E) // BLK
N_LOOP = (NBLK - 2) // 6
N_TAIL = NBLK - 6 * N_LOOP
SLOTS = PAIRS + BLK
NEG = -1e30
TAKEN = float(np.float32(-3e38))
EPS = 1e-6
SCALE = DH ** -0.5
GELU_C = 0.7978845608028654

ZOFF, _o = {}, 0
for _n, _w in (("q_a", W), ("k_cmp", DH), ("v_cmp", DH), ("k_sel", DH), ("v_sel", DH), ("k_win", DH),
               ("v_win", DH), ("g_a", H * 3), ("q_b", W), ("k_b", W), ("v_b", W), ("f_b", H), ("q_c", W),
               ("ckv", P), ("q_i", W), ("k_i", DH), ("w_i", H), ("q_d", W), ("k_d", 2 * DH), ("v_d", 2 * DH)):
    ZOFF[_n] = _o
    _o += _w
D_IN = _o
NZ = -(-D_IN // 512)

CONST = {}
_c = 0
for _n, _w in (("ident", P), ("causal", T), ("swa", T), ("cmp", NT * N_CMP), ("cmp_row", NT), ("before", P),
               ("upto", P), ("ones", P), ("inv_freq", 32), ("slot", PAIRS), ("block", NBLK), ("expert", 1),
               ("eye8", H), ("rank8", GROUPS), ("rank64", E)):
    CONST[_n] = (_c, _w)
    _c += _w
N_CONST = _c


def constants():
    c = np.zeros((P, N_CONST), np.float32)

    def put(name, v):
        o, w = CONST[name]
        c[:, o:o + w] = np.asarray(v, np.float32).reshape(P, w)

    p = np.arange(P)[:, None]
    put("ident", np.eye(P))
    t = p[:, :, None] + P * np.arange(NT)[None, :, None]
    s = np.arange(T)[None, None, :]
    last = t[:, 1:2]
    put("causal", np.where(s <= last, 0.0, NEG))
    put("swa", np.where((s <= last) & (last - s < SWA_WIN), 0.0, NEG))
    seen = CMP_STRIDE * np.arange(N_CMP)[None, None, :] + CMP_LEN - 1 <= t
    put("cmp", np.where(seen, 0.0, NEG))
    put("cmp_row", seen.any(-1))
    put("before", p < np.arange(P)[None])
    put("upto", p <= np.arange(P)[None])
    put("ones", np.ones((P, P)))
    put("inv_freq", np.broadcast_to(10000.0 ** (-np.arange(32) / 32.0), (P, 32)))
    put("slot", np.broadcast_to(np.arange(PAIRS), (P, PAIRS)))
    put("block", np.broadcast_to(np.arange(NBLK), (P, NBLK)))
    put("expert", p)
    put("eye8", 8.0 * np.eye(P)[:, :H])
    put("rank8", np.broadcast_to(GROUPS - np.arange(GROUPS), (P, GROUPS)))
    put("rank64", np.broadcast_to(E - np.arange(E), (P, E)))
    return c


ROPE = [(ZOFF["k_sel"], 2, 2 * DH), (ZOFF["q_a"], 5, DH), (ZOFF["q_c"], 4, DH), (ZOFF["q_i"], 5, DH),
        (ZOFF["q_d"], 6, DH)]
SRC = {"qb0": (ZOFF["q_b"], 0), "qb1": (ZOFF["q_b"] + P, 0), "kb0": (ZOFF["k_b"], 0), "kb1": (ZOFF["k_b"] + P, 0),
       "qi0": (ZOFF["q_i"], 0), "qi1": (ZOFF["q_i"] + P, 0), "ki": (ZOFF["k_i"], 1), "kvcmp": (ZOFF["k_cmp"], 0),
       "qa0": (ZOFF["q_a"], 0), "qa1": (ZOFF["q_a"] + P, 0), "ksel": (ZOFF["k_sel"], 1), "kwin": (ZOFF["k_win"], 1),
       "qc0": (ZOFF["q_c"], 0), "qc1": (ZOFF["q_c"] + P, 0), "qd0": (ZOFF["q_d"], 0), "qd1": (ZOFF["q_d"] + P, 0),
       "kd0": (ZOFF["k_d"], 1), "kd1": (ZOFF["k_d"] + DH, 1)}
SRCS = list(SRC)
TWINS = ["ki", "ksel", "kwin", "kd0", "kd1"]
TSLOT = {n: i for i, n in enumerate(SRCS)}
TSLOT.update(ckv=18, kc0=20, kc1=21)
NTS = 22

UNITS = [(m, t) for m in ("fox", "sel", "win", "cmp", "swa", "dsa") for t in range(NT)]
OUT_OF = {"sel": 0, "win": 0, "cmp": 0, "fox": 1, "dsa": 2, "swa": 3}
GATE_OF = {"cmp": 0, "sel": 1, "win": 2}

ITEMS = ([("win", n) for n in range(NZ)] + [("gate", 0), ("gate", 1), ("w1", 0), ("w1", 1)]
         + [("gate", n) for n in range(2, 8)] + [("wb", 0), ("wb", 1), ("wo", 0), ("wo", 1)])
ITEM = {n: i for i, n in enumerate(ITEMS)}
NRING = 4
ARRIVED, _cnt = {}, [0] * NRING
for _i, _n in enumerate(ITEMS):
    _cnt[_i % NRING] += 32 if _n[0] == "w1" else 16
    ARRIVED[_n] = _cnt[_i % NRING]

T_USE = (["pe"] + [("hn", t, g) for t in range(NT) for g in range(2)] + [("src", i) for i in range(4)]
         + ["ckv"] + [("src", i) for i in range(4, 9)] + ["kc", "cmph"]
         + [("p", u, i) for u, (m, t) in enumerate(UNITS) for i in range(2 if t and m != "cmp" else 1)]
         + [("o", i) for i in range(4)] + [("m", t, g) for t in range(NT) for g in range(2)]
         + [("hn2", t, g) for t in range(NT) for g in range(2)] + [("st", i) for i in range(2)]
         + [("y", s, g) for s in range(4) for g in range(2)])
T_AT = {n: i for i, n in enumerate(T_USE)}
G_USE = (["bc"] + [("z", n) for n in range(NZ)] + ["cum", ("idx", 0), ("idx", 1), "kvc", "cmph", "cmpo"]
         + [("s", u) for u in range(len(UNITS))] + [("mg", t, n, i) for t in range(NT) for n in range(2) for i in range(2)]
         + [("wo", t) for t in range(NT)] + ["router", "tot", "pos", "blk"] + [("ga", i) for i in range(4)]
         + [("sc", t) for t in range(NT)])
G_AT = {n: i for i, n in enumerate(G_USE)}
GATES = [(n, t) for n in range(8) for t in range(NT)]

LAYER_SEMS = ("wfree", "small", "small2", "wr", "ss", "ms", "rms", "hn", "hnt", "tp", "te0", "te1", "g", "ge0", "ge1", "dve",
              "gate", "gate_out", "rope", "twin", "foxneg", "foxexp", "foxln", "logf", "sm", "exp", "sink", "sinkexp",
              "pv", "oc", "relu", "ckvss", "ckvms", "ckvrms", "ckvn", "kvrope", "zc", "gelu_in", "gelu_b",
              "gelu_th", "gelu", "ln_e", "logits", "gexp_in", "gexp", "texp_in", "texp", "oh", "cnt", "pos", "blk3",
              "tab", "p01", "pw", "pad", "gu", "th", "hid_a", "hid", "hid_t", "hidT", "whi", "wlo", "xh", "xl", "down", "ya", "yd",
              "ss2", "ms2", "rms2", "hn2", "h")
ALL_SEMS = LAYER_SEMS + tuple(f"w{i}" for i in range(NRING)) + tuple(
    f"e{k}{i}" for k in ("g", "u", "d") for i in range(3))


def trunk(nc, A, out):
    with ExitStack() as ctx:
        base = nc.sbuf_base
        place = {}

        def sb(name, shape, dt=F32):
            place[name] = nc.sbuf_base
            return ctx.enter_context(nc.sbuf_tensor(name, shape, dt))

        def over(name, what, shape, dt=F32R, skip=0):
            return nc.alloc_sbuf_tensor_at(name, shape, dt, offset=place[what] + skip)

        h = sb("h", [P, NT, D])
        hn = sb("hn", [P, NT, D])
        hnT = sb("hnT", [P, KC, T])
        zx = sb("zx", [P, 5288])
        ty = sb("ty", [P, NTS * T])
        gt = sb("gt", [P, NT, 4, D])
        ring = sb("ring", [P, 3 * 6144])
        ptb = sb("ptb", [P, 1024])
        kvs = sb("kvs", [P, NT, 2 * W])
        oall = sb("oall", [P, NT, 4, W])
        sel = sb("sel", [P, NT, T])
        cst = sb("cst", [P, N_CONST])
        cos = sb("cos", [P, NT, DH])
        sin = sb("sin", [P, NT, DH])
        otmp = sb("otmp", [P, W])
        wr = sb("wr", [P, KC, GROUPS + E])
        row = sb("row", [1, 80])
        bc = sb("bc", [P, 80])
        gain1 = sb("gain1", [P, KC])
        gain2 = sb("gain2", [P, KC])
        ckvg = sb("ckvg", [P, 1])
        pe_in = sb("pe_in", [CMP_LEN, P])
        peT = sb("peT", [P, CMP_LEN])
        small = sb("small", [P, 512])
        nmx = sb("nmx", [P, 14, H])
        ssum = sb("ssum", [P, 14, H])
        tab = sb("tab", [1, 2, NBLK], I32)
        tabf = sb("tabf", [1, 2, NBLK])

        w_hi = [over(f"w_hi{i}", "gt", [P, 2, KC, DE], skip=16384 * i) for i in range(2)]
        w_lo = [over(f"w_lo{i}", "ring", [P, 2, KC, DE], skip=24576 * i) for i in range(3)]
        x_hi = [over(f"x_hi{i}", w, [P, KC, BLK]) for i, w in enumerate(("hnT", "oall"))]
        x_lo = [over(f"x_lo{i}", w, [P, KC, BLK], skip=4096) for i, w in enumerate(("hnT", "oall"))]

        psT = ctx.enter_context(nc.psum_tensor("psT", [P, 2, 512], F32))
        psG = ctx.enter_context(nc.psum_tensor("psG", [P, 2, 2, 512], F32))
        psO = ctx.enter_context(nc.psum_tensor("psO", [P, 2, W], F32))
        psA = ctx.enter_context(nc.psum_tensor("psA", [P, 512], F32))

        S = {n: ctx.enter_context(nc.semaphore("s_" + n)) for n in ALL_SEMS}
        s_pre = {n: ctx.enter_context(nc.semaphore("p_" + n)) for n in ("dma", "pos", "dve", "ang", "sin", "out",
                                                                       "ss", "ms", "rms", "g", "fin", "y")}

        def C(name):
            o, w = CONST[name]
            return cst[:, o:o + w]

        ident, ones = C("ident"), C("ones")
        causal = [C("causal")[:, P:T], C("causal")]
        swa_mask = [C("causal")[:, P:T], C("swa")]
        cmp_mask = [C("cmp")[:, N_CMP * t:N_CMP * (t + 1)] for t in range(NT)]
        z = zx[:, 0:NT * D_IN].rearrange("p (t n) -> p t n", t=NT)
        xs = zx[:, 0:KC * SLOTS].rearrange("p (k s) -> p k s", k=KC)
        tr = ty[:, :].rearrange("p (n t) -> p n t", t=T)
        oT = ty[:, 0:4 * 2 * T].rearrange("p (i c t) -> p i c t", i=4, c=2)
        yT = ty[:, 0:KC * SLOTS].rearrange("p (k s) -> p k s", k=KC)
        yn = gt[:, :, :, :].rearrange("p a b n -> p (a b n)")[:, 0:4 * D].rearrange("p (s n) -> p s n", s=4)
        ukv = gt[:, 1, 3, 512:1024]
        w2k = gt[:, 0, 3, 512:768].rearrange("p (c a d) -> p c a d", c=2, a=2)
        w2v = gt[:, 0, 3, 768:896].rearrange("p (c d) -> p c d", c=2)
        twin = gt[:, 1, 2:4].rearrange("p i n -> p (i n)")[:, 0:NT * len(TWINS) * 2 * DH].rearrange(
            "p (t n d) -> p t n d", t=NT, n=len(TWINS))
        zc = oall[:, 1].rearrange("p i w -> p (i w)")[:, 0:CMP_LEN * N_CMP].rearrange("p (l c) -> p l c", l=CMP_LEN)
        fin = ring[0:1, 0:D]
        slot16 = [ring[:, 4096 * i:4096 * (i + 1)] for i in range(NRING)]
        eslot = [ring[:, 6144 * i:6144 * (i + 1)] for i in range(3)]
        sm = [hn[:, i, :].rearrange("p (h s) -> p h s", h=H) for i in range(2)]
        merged = hn
        pt = ptb[:, :].rearrange("p (h k q) -> p h k q", h=H, k=NT)
        mtmp = ptb[:, 0:512]
        stt_ = kvs[:, :, :].rearrange("p a b -> p (a b)").rearrange("p (s t) -> p s t", s=4)
        onehot = oall[:, 0].rearrange("p i w -> p (i w)").rearrange("p (t s) -> p t s", t=NT)
        weighted = oall[:, 1].rearrange("p i w -> p (i w)").rearrange("p (t s) -> p t s", t=NT)
        th, hida = (hn[:, 0, 512 * i:512 * i + 512].rearrange("p (b n) -> p b n", b=2) for i in range(2))
        hid = hn[:, 1, 0:512].rearrange("p (b n) -> p b n", b=2)
        hidT = hn[:, 1, 512:1024].rearrange("p (b j s) -> p b j s", b=2, j=2)
        psH = [psO[:, :, :].rearrange("p a b -> p (a b)")[:, 0:2 * BLK], psA[:, 0:2 * BLK]]

        _s = [0]

        def sm_(n):
            _s[0] += n
            return small[:, _s[0] - n:_s[0]]

        ss, rms, rstd = sm_(2), sm_(2), sm_(2)
        css, crms, crstd = sm_(2), sm_(2), sm_(2)
        fx = sm_(8).rearrange("p (t h) -> p t h", t=2)
        fa = sm_(8).rearrange("p (t h) -> p t h", t=2)
        logf = sm_(8).rearrange("p (t h) -> p t h", t=2)
        wi = sm_(8).rearrange("p (t h) -> p t h", t=2)
        ga = sm_(24).rearrange("p (t h g) -> p t h g", t=2, h=H)
        m8 = sm_(8)
        coef, sinkv = sm_(H), sm_(H)
        coef2 = sm_(H)
        gmx, pg, v1, v2, ee, w1s, w2s, d1, d2 = (sm_(2) for _ in range(9))
        g8 = sm_(16).rearrange("p (t g) -> p t g", t=2)
        g8b = sm_(16).rearrange("p (t g) -> p t g", t=2)
        ohg = sm_(16).rearrange("p (t g) -> p t g", t=2)
        cnt, pos = sm_(2), sm_(2)
        bend, c0 = sm_(1), sm_(1)
        kcT = sm_(N_CMP)
        hcT = sm_(4 * N_CMP).rearrange("p (j c) -> p j c", j=4)
        cumT, ncumT = kvs[0:H, 0, 0:T], kvs[0:H, 0, T:2 * T]
        vc = kvs[0:N_CMP, 1, 0:DH]
        gx, gb = oall[0:N_CMP, 0, 0:2].rearrange("p i w -> p (i w)"), oall[0:N_CMP, 0, 2:4].rearrange("p i w -> p (i w)")
        vcs = sb("vcs", [N_CMP, DH])
        cumb = sb("cumb", [H, 2, T])
        lg = ptb[:, 0:144].rearrange("p (t n) -> p t n", t=2)
        em = ptb[:, 144:272].rearrange("p (t n) -> p t n", t=2)
        eq = ptb[:, 272:400].rearrange("p (t n) -> p t n", t=2)
        oh1 = ptb[:, 400:528].rearrange("p (t n) -> p t n", t=2)
        oh2 = ptb[:, 528:656].rearrange("p (t n) -> p t n", t=2)
        oh = ptb[:, 656:784].rearrange("p (t n) -> p t n", t=2)
        totbc = ptb[0:E, 784:912]
        blk3 = sel[0:E, :, :].rearrange("p a b -> p (a b)")[:, 0:3 * NBLK].rearrange("p (a b) -> p a b", a=3)

        AT = [0, 2, 1, 3]

        def by_head(a):
            return a.rearrange("p (a b) -> p b a", a=2)

        def pt_of(kt, x, s):
            j = x if kt == 1 else 2 * x + s
            return ptb[:, P * j:P * (j + 1)]

        def T_use(pe, name):
            i = T_AT[name]
            if i >= 2:
                pe.wait_ge(S[f"te{i % 2}"], i // 2)
            return psT[:, i % 2, :]

        def T_ready(eng, name):
            i = T_AT[name]
            eng.wait_ge(S["tp"], i + 1)
            return psT[:, i % 2, :], S[f"te{i % 2}"]

        def G_use(pe, name):
            i = G_AT[name]
            if i >= 2:
                pe.wait_ge(S[f"ge{i % 2}"], i // 2)
            return psG[:, i % 2]

        def G_ready(eng, name):
            i = G_AT[name]
            eng.wait_ge(S["g"], i + 1)
            return psG[:, i % 2], S[f"ge{i % 2}"]

        def T_out_upto(eng, name):
            for b in range(2):
                eng.wait_ge(S[f"te{b}"], (T_AT[name] - b) // 2 + 1)

        def G_out_upto(eng, name):
            for b in range(2):
                eng.wait_ge(S[f"ge{b}"], (G_AT[name] - b) // 2 + 1)

        def arrived(i, d):
            return 32 * i + 16 * (d // 3 + 1)

        def item(pe, name):
            i = ITEM[name]
            pe.wait_ge(S[f"w{i % NRING}"], ARRIVED[name])
            return slot16[i % NRING]

        posi = small[:, 500:502].bitcast(I32)
        posf = small[:, 502:504]
        ang = ptb[:, 0:64].rearrange("p (t f) -> p t f", t=NT)
        kk = ptb[:, 64:128].rearrange("p (t f) -> p t f", t=NT)
        sn = ptb[:, 128:192].rearrange("p (t f) -> p t f", t=NT)
        sh = ptb[:, 192:256].rearrange("p (t f) -> p t f", t=NT)

        with nc.Block() as block:
            @block.sync
            def _(sp):
                sp.dma_start(cst[:, :], A["consts"]).then_inc(s_pre["dma"], 16)
                for t in range(NT):
                    sp.dma_start(posi[:, t:t + 1], A["positions"][0:1, t * P:(t + 1) * P].rearrange("a p -> p a")
                                 ).then_inc(s_pre["dma"], 16)
                sp.dma_start(h[:, :, :], A["x"][0].rearrange("(t p) d -> p t d", p=P)).then_inc(s_pre["dma"], 16)
                sp.wait_ge(s_pre["dma"], 64)

            @block.vector
            def _(dve):
                n = [0]

                def link(ins):
                    n[0] += 1
                    ins.then_inc(s_pre["dve"], 1)
                    dve.wait_ge(s_pre["dve"], n[0])

                dve.wait_ge(s_pre["dma"], 64)
                link(dve.tensor_copy(posf, posi))
                for t in range(NT):
                    link(dve.tensor_scalar(ang[:, t], C("inv_freq"), posf[:, t:t + 1], None, ALU.mult))
                magic, two_pi = 12582912.0, 2 * np.pi
                c1 = 6.28125
                c2 = float(np.float32(np.round((two_pi - c1) * 2 ** 20) / 2 ** 20))
                c3 = float(np.float32(two_pi - c1 - c2))
                link(dve.tensor_scalar(kk, ang, 1 / two_pi, magic, ALU.mult, ALU.add))
                link(dve.tensor_scalar(kk, kk, -magic, None, ALU.add))
                for c in (c1, c2, c3):
                    link(dve.scalar_tensor_tensor(out=ang, in0=kk, scalar=-c, in1=ang, op0=ALU.mult, op1=ALU.add))
                dve.tensor_scalar(ang, ang, 3.1415925, -3.1415925, ALU.min, ALU.max).then_inc(s_pre["ang"], 1)
                dve.wait_ge(s_pre["sin"], 2)
                link(dve.tensor_tensor(kk, sh, sh, ALU.mult))
                for half in range(2):
                    link(dve.tensor_scalar(cos[:, :, 32 * half:32 * half + 32], kk, -2.0, 1.0, ALU.mult, ALU.add))
                link(dve.tensor_scalar(sin[:, :, 0:32], sn, -1.0, None, ALU.mult))
                link(dve.tensor_copy(sin[:, :, 32:64], sn))

            @block.scalar
            def _(act):
                act.wait_ge(s_pre["ang"], 1)
                act.activation(sn, ang, ACT.Sin).then_inc(s_pre["sin"], 1)
                act.activation(sh, ang, ACT.Sin, scale=0.5).then_inc(s_pre["sin"], 1)

        with nc.Fori(0, DEPTH) as l:
            def at(name):
                a = A[name]
                return a[bass.ds(l, 1)]

            with nc.Block() as block:
                @block.sync
                def _(sp):
                    def small_load(dst, src, s="small"):
                        sp.dma_start(dst, src).then_inc(S[s], 16)

                    def load_item(i):
                        kind, n = ITEMS[i]
                        dst, s = slot16[i % NRING], S[f"w{i % NRING}"]
                        if i >= NRING:
                            sp.wait_ge(S["wfree"], i - NRING + 1)
                        if kind == "win":
                            c = min(512, D_IN - 512 * n)
                            sp.dma_start(dst[:, 0:KC * c].rearrange("p (k n) -> p k n", k=KC),
                                         at("w_in")[:, :, 512 * n:512 * n + c].rearrange("l (p k) n -> (l p) k n", k=KC)
                                         ).then_inc(s, 16)
                        elif kind == "gate":
                            b, c = n // 2, 512 * (n % 2)
                            sp.dma_start(dst.rearrange("p (k n) -> p k n", k=KC),
                                         at("w_gate")[:, b, :, c:c + 512].rearrange("l (p k) n -> (l p) k n", k=KC)
                                         ).then_inc(s, 16)
                        elif kind == "w1":
                            for j, name in enumerate(("nsa_w1_k", "nsa_w1_v")):
                                sp.dma_start(dst[DH * j:DH * (j + 1), :].rearrange("d (l n) -> d l n", n=CMP_HID),
                                             at(name).rearrange("l (c d) n -> (l d) c n", d=DH)[:, 16 * n:16 * n + 16, :]
                                             ).then_inc(s, 16)
                        elif kind == "wb":
                            sp.dma_start(dst.rearrange("p (i c n) -> p i c n", i=2, c=2),
                                         at("w_branch")[:, 2 * n:2 * n + 2].rearrange("l i (c p) n -> (l p) i c n", p=P)
                                         ).then_inc(s, 16)
                        else:
                            sp.dma_start(dst.rearrange("p (k n) -> p k n", k=KC),
                                         at("w_out")[:, :, 512 * n:512 * n + 512].rearrange("l (p k) n -> (l p) k n", k=KC)
                                         ).then_inc(s, 16)

                    small_load(gain1[:, :], at("attn_norm").rearrange("l (p k) -> (l p) k", k=KC))
                    load_item(0)
                    small_load(row[0:1, 0:8], at("moe_b_group"))
                    small_load(row[0:1, 8:72], at("moe_b_expert"))
                    small_load(row[0:1, 72:76], at("fox_forget_bias"))
                    small_load(row[0:1, 76:80], at("swa_sinks"))
                    small_load(pe_in[:, 0:DH], at("nsa_pe_k").rearrange("l c d -> (l c) d"))
                    small_load(pe_in[:, DH:2 * DH], at("nsa_pe_v").rearrange("l c d -> (l c) d"))
                    for i in range(1, NRING):
                        load_item(i)
                    small_load(gain2[:, :], at("ffn_norm").rearrange("l (p k) -> (l p) k", k=KC), "small2")
                    small_load(ckvg[:, :], at("dsa_kv_norm").rearrange("l (p a) -> (l p) a", a=1), "small2")
                    small_load(ukv[:, :], at("dsa_w_ukv").rearrange("l p n -> (l p) n"), "small2")
                    for j in range(2):
                        small_load(w2k[:, :, j, :], at("nsa_w2_k").rearrange("l (c p) d -> (l p) c d", p=P), "small2")
                    small_load(w2v[:, :, :], at("nsa_w2_v").rearrange("l (c p) d -> (l p) c d", p=P), "small2")
                    small_load(wr[:, :, 0:GROUPS], at("moe_w_group").rearrange("l (p k) n -> (l p) k n", k=KC), "small2")
                    small_load(wr[:, :, GROUPS:], at("moe_w_expert").rearrange("l (p k) n -> (l p) k n", k=KC), "small2")
                    for i in range(NRING, len(ITEMS)):
                        load_item(i)

                    def load_block(b, j, wait=None):
                        e = sp.value_load(tab[0:1, 0, bass.ds(b, 1)], min_val=0, max_val=E - 1)
                        for k, (name, r) in enumerate((("moe_w_gate", KC), ("moe_w_up", KC), ("moe_w_down", 2))):
                            if wait is not None and k == 0:
                                sp.wait_ge(S["gu"], wait)
                            if wait is not None and k == 2:
                                sp.wait_ge(S["down"], wait)
                            src = A[name][bass.ds(l, 1), bass.ds(e, 1)].rearrange("l e (p k) n -> (l e p) (k n)", k=r)
                            sp.dma_start(eslot[j][:, 2048 * k:2048 * (k + 1)], src).then_inc(S[f"e{'gud'[k]}{j}"], 16)

                    sp.wait_ge(S["tab"], 1)
                    sp.wait_ge(S["wfree"], len(ITEMS))
                    for j in range(3):
                        load_block(j, j)
                    with sp.Fori(1, NBLK // 3) as i:
                        for j in range(3):
                            load_block(3 * i + j, j, 3 * i + (j - 2))
                    for b in range(NBLK // 3 * 3, NBLK):
                        load_block(b, b % 3, b - 2)

                @block.tensor
                def _(pe):
                    def transposes(name, ins):
                        bank = T_use(pe, name)
                        w = 0
                        for a in ins:
                            n = a.shape[0]
                            m = pe.transpose(bank[0:a.shape[-1], w:w + n], a, ident[0:n, 0:n])
                            w += P if n == P else N_CMP if n == N_CMP else n
                        m.then_inc(S["tp"], 1)

                    gate_at = [0]

                    def gate_units(n):
                        for _ in range(n):
                            if gate_at[0] == len(GATES):
                                return
                            i, t = GATES[gate_at[0]]
                            w = item(pe, ("gate", i)).rearrange("p (k n) -> p k n", k=KC)
                            if gate_at[0]:
                                pe.wait_ge(S["gate_out"], gate_at[0])
                            for k in range(KC):
                                m = pe.matmul(psA[:, :], hnT[:, k, t * P:(t + 1) * P], w[:, k, :],
                                              start=(k == 0), stop=(k == KC - 1))
                            m.then_inc(S["gate"], 1)
                            gate_at[0] += 1
                            if t == NT - 1:
                                release(m)

                    def release(m):
                        pe.wait_ge(S["gate"], gate_at[0])
                        pe.sem_inc(S["wfree"], 1)

                    pe.wait_ge(S["small"], 16 * 7)
                    transposes("pe", [pe_in[:, :]])
                    g = G_use(pe, "bc")
                    pe.matmul(g[:, 0, 0:80], ones[0:1, :], row[0:1, :], start=True, stop=True).then_inc(S["g"], 1)
                    for t in range(NT):
                        pe.wait_ge(S["hn"], t + 1)
                        for q in range(2):
                            transposes(("hn", t, q), [hn[:, t, k:D:KC] for k in range(4 * q, 4 * q + 4)])
                    pe.wait_ge(S["hnt"], 4)
                    for n in range(NZ):
                        c = min(512, D_IN - 512 * n)
                        w = item(pe, ("win", n))[:, 0:KC * c].rearrange("p (k n) -> p k n", k=KC)
                        g = G_use(pe, ("z", n))
                        for t in range(NT):
                            for k in range(KC):
                                m = pe.matmul(g[:, t, 0:c], hnT[:, k, t * P:(t + 1) * P], w[:, k, :],
                                              start=(k == 0), stop=(k == KC - 1))
                        m.then_inc(S["g"], 1)
                        pe.wait_ge(S["g"], G_AT[("z", n)] + 1)
                        pe.sem_inc(S["wfree"], 1)

                    def head_T(name, t=None):
                        a = tr[:, TSLOT[name], :]
                        return a if t is None else a[:, t * P:(t + 1) * P]

                    def src(name, t):
                        c, twice = SRC[name]
                        if twice:
                            return twin[:, t, TWINS.index(name), :]
                        return z[:, t, c:c + P]

                    def src_T(i):
                        bank = T_use(pe, ("src", i))
                        w = 0
                        for name in SRCS[2 * i:2 * i + 2]:
                            for t in range(NT):
                                m = pe.transpose(bank[:, w:w + P], src(name, t), ident)
                                w += P
                        m.then_inc(S["tp"], 1)

                    gate_units(2)
                    G_out_upto(pe, ("z", NZ - 1))
                    src_T(0)
                    src_T(1)
                    pe.wait_ge(S["logf"], 1)
                    g = G_use(pe, "cum")
                    pe.matmul(g[0:H, 0, 0:P], logf[:, 0, :], C("upto"), start=True, stop=True)
                    pe.matmul(g[0:H, 1, 0:P], logf[:, 0, :], ones, start=True, stop=False)
                    pe.matmul(g[0:H, 1, 0:P], logf[:, 1, :], C("upto"), start=False, stop=True).then_inc(S["g"], 1)
                    gate_units(1)
                    pe.wait_ge(S["rope"], 2)
                    src_T(2)
                    pe.wait_ge(S["twin"], 1)
                    src_T(3)

                    def scores(g, t, q, k, w):
                        for x in range(H):
                            lo = DH * (x % 2)
                            m = pe.matmul(g[:, x % 2, T * (x // 2):T * (x // 2) + w],
                                          head_T(q[x // 2], t)[lo:lo + DH, :], k(x)[lo:lo + DH, 0:w], start=True, stop=True)
                        return m

                    T_out_upto(pe, ("src", 3))
                    for t in range(NT):
                        g = G_use(pe, ("idx", t))
                        scores(g, t, ("qi0", "qi1"), lambda x: head_T("ki"), P * (t + 1)).then_inc(S["g"], 1)
                    pe.wait_ge(S["ckvn"], 1)
                    pe.wait_ge(S["small2"], 16 * 8)
                    transposes("ckv", [kvs[:, t, 0:P] for t in range(NT)])
                    gate_units(1)
                    T_out_upto(pe, "ckv")
                    g = G_use(pe, "kvc")
                    for t in range(NT):
                        m = pe.matmul(g[:, t, :], head_T("ckv", t), ukv[:, :], start=True, stop=True)
                    m.then_inc(S["g"], 1)
                    pe.wait_ge(S["twin"], len(TWINS))
                    for i in range(4, 9):
                        src_T(i)
                    pe.wait_ge(S["kvrope"], 1)
                    bank = T_use(pe, "kc")
                    for i in range(2):
                        for t in range(NT):
                            m = pe.transpose(bank[:, P * (2 * i + t):P * (2 * i + t + 1)], kvs[:, t, P * i:P * (i + 1)],
                                             ident)
                    m.then_inc(S["tp"], 1)
                    pe.wait_ge(S["zc"], 1)
                    g = G_use(pe, "cmph")
                    for n in range(2):
                        w = item(pe, ("w1", n)).rearrange("p (l n) -> p l n", n=CMP_HID)
                        for j in range(2):
                            for c in range(16):
                                m = pe.matmul(g[0:N_CMP, j, 0:CMP_HID], zc[DH * j:DH * (j + 1), 16 * n + c, :],
                                              w[DH * j:DH * (j + 1), c, :], start=(n == 0 and c == 0),
                                              stop=(n == 1 and c == 15))
                        if n:
                            m.then_inc(S["g"], 1)
                            pe.wait_ge(S["g"], G_AT["cmph"] + 1)
                            pe.sem_inc(S["wfree"], 2)
                    gate_units(2)
                    pe.wait_ge(S["gelu"], 1)
                    transposes("cmph", [gx[:, P * j:P * (j + 1)] for j in range(4)])
                    T_out_upto(pe, "cmph")
                    g = G_use(pe, "cmpo")
                    for c in range(2):
                        pe.matmul(g[:, 0, 0:N_CMP], w2k[:, c].rearrange("p a d -> p (a d)"), hcT[:, c, :],
                                  start=(c == 0), stop=(c == 1))
                    for c in range(2):
                        m = pe.matmul(g[0:N_CMP, 1, 0:DH], hcT[:, 2 + c, :], w2v[:, c, :],
                                      start=(c == 0), stop=(c == 1))
                    m.then_inc(S["g"], 1)

                    def unit_scores(u):
                        m_, t = UNITS[u]
                        w = P * (t + 1)
                        g = G_use(pe, ("s", u))
                        if m_ == "fox":
                            for x in range(H):
                                lo = DH * (x % 2)
                                o = g[:, x % 2, T * (x // 2):T * (x // 2) + w]
                                pe.matmul(o, head_T(f"qb{x // 2}", t)[lo:lo + DH, :],
                                          head_T(f"kb{x // 2}")[lo:lo + DH, 0:w], start=True, stop=False)
                                e8 = C("eye8")[0:H, x:x + 1]
                                pe.matmul(o, cumb[:, 0, t * P:(t + 1) * P], e8.broadcast_to([H, w]),
                                          start=False, stop=False)
                                m = pe.matmul(o, e8.broadcast_to([H, P]), cumb[:, 1, 0:w], start=False, stop=True)
                        elif m_ == "cmp":
                            for x in range(H):
                                lo = DH * (x % 2)
                                m = pe.matmul(g[:, x % 2, T * (x // 2):T * (x // 2) + N_CMP],
                                              head_T(f"qa{x // 2}", t)[lo:lo + DH, :], kcT[lo:lo + DH, :],
                                              start=True, stop=True)
                        else:
                            q = {"sel": "qa", "win": "qa", "swa": "qd", "dsa": "qc"}[m_]
                            k = {"sel": lambda x: head_T("ksel"), "win": lambda x: head_T("kwin"),
                                 "swa": lambda x: head_T(f"kd{x // 2}"), "dsa": lambda x: head_T(f"kc{x // 2}")}[m_]
                            m = scores(g, t, (q + "0", q + "1"), k, w)
                        m.then_inc(S["g"], 1)

                    def unit_pt(u):
                        m_, t = UNITS[u]
                        pe.wait_ge(S["exp"], H * (u + 1))
                        kt = NT if t and m_ != "cmp" else 1
                        w = N_CMP if m_ == "cmp" else P
                        for i in range(kt):
                            bank = T_use(pe, ("p", u, i))
                            for j in range(4):
                                x, s = (j, 0) if kt == 1 else (2 * i + j // 2, j % 2)
                                mm = pe.transpose(bank[0:w, P * j:P * (j + 1)], sm[u % 2][:, AT[x], P * s:P * s + w], ident)
                            mm.then_inc(S["tp"], 1)
                        return kt

                    def unit_pv(u, kt):
                        m_, t = UNITS[u]
                        if u:
                            pe.wait_ge(S["oc"], u)
                        i = T_AT[("p", u, kt - 1)]
                        for j in range(kt):
                            pe.wait_ge(S[f"te{(i - j) % 2}"], (i - j) // 2 + 1)
                        for x in range(H):
                            for s in range(kt):
                                if m_ == "fox":
                                    v = z[:, s, ZOFF["v_b"] + DH * x:ZOFF["v_b"] + DH * (x + 1)]
                                elif m_ == "swa":
                                    c = ZOFF["v_d"] + DH * (x // 2)
                                    v = z[:, s, c:c + DH]
                                elif m_ == "dsa":
                                    v = kvs[:, s, W + DH * x:W + DH * (x + 1)]
                                elif m_ == "cmp":
                                    v = vcs[:, :]
                                else:
                                    c = ZOFF["v_" + m_]
                                    v = z[:, s, c:c + DH]
                                w = N_CMP if m_ == "cmp" else P
                                lhs = pt_of(kt, x, s)[0:w]
                                mm = pe.matmul(psO[:, u % 2, DH * x:DH * (x + 1)], lhs, v, start=(s == 0), stop=(s == kt - 1))
                        mm.then_inc(S["pv"], 1)

                    NU = len(UNITS)
                    T_out_upto(pe, "kc")
                    G_out_upto(pe, "cmpo")
                    unit_scores(0)
                    for u in range(NU):
                        if u + 1 < NU:
                            unit_scores(u + 1)
                        gate_units(1)
                        unit_pv(u, unit_pt(u))
                    gate_units(16)
                    pe.wait_ge(S["oc"], NU)
                    for i in range(4):
                        transposes(("o", i), [oall[:, t, i, P * c:P * (c + 1)] for c in range(2) for t in range(NT)])
                    T_out_upto(pe, ("o", 3))
                    for t in range(NT):
                        for n in range(2):
                            for i2 in range(2):
                                w = item(pe, ("wb", i2)).rearrange("p (i c n) -> p i c n", i=2, c=2)
                                g = G_use(pe, ("mg", t, n, i2))
                                for j in range(2):
                                    for c in range(2):
                                        m = pe.matmul(g[:, j, :], oT[:, 2 * i2 + j, c, t * P:(t + 1) * P],
                                                      w[:, j, c, 512 * n:512 * n + 512], start=(c == 0), stop=(c == 1))
                                m.then_inc(S["g"], 1)
                    for t in range(NT):
                        G_out_upto(pe, ("mg", t, 1, 1))
                        for q in range(2):
                            transposes(("m", t, q), [merged[:, t, k:D:KC] for k in range(4 * q, 4 * q + 4)])
                    T_out_upto(pe, ("m", 1, 1))
                    for t in range(NT):
                        g = G_use(pe, ("wo", t))
                        for n in range(2):
                            w = item(pe, ("wo", n)).rearrange("p (k n) -> p k n", k=KC)
                            for k in range(KC):
                                m = pe.matmul(g[:, n, :], hnT[:, k, t * P:(t + 1) * P], w[:, k, :],
                                              start=(k == 0), stop=(k == KC - 1))
                        m.then_inc(S["g"], 1)
                    pe.wait_ge(S["g"], G_AT[("wo", 1)] + 1)
                    pe.sem_inc(S["wfree"], 4)

                    for t in range(NT):
                        pe.wait_ge(S["hn2"], t + 1)
                        for q in range(2):
                            transposes(("hn2", t, q), [hn[:, t, k:D:KC] for k in range(4 * q, 4 * q + 4)])
                    pe.wait_ge(S["hnt"], 8)
                    g = G_use(pe, "router")
                    for t in range(NT):
                        for k in range(KC):
                            pe.matmul(g[:, t, 0:GROUPS + E], hnT[:, k, t * P:(t + 1) * P], wr[:, k, :],
                                      start=(k == 0), stop=False)
                        m = pe.matmul(g[:, t, 0:GROUPS + E], ones[0:1, :], row[0:1, 0:GROUPS + E], start=False, stop=True)
                    m.then_inc(S["g"], 1)
                    pe.wait_ge(S["oh"], 1)
                    g = G_use(pe, "tot")
                    for t in range(NT):
                        m = pe.matmul(g[0:E, 0, 0:1], oh[:, t, :], ones[:, 0:1], start=(t == 0), stop=(t == NT - 1))
                    m.then_inc(S["g"], 1)
                    pe.wait_ge(S["cnt"], 1)
                    g = G_use(pe, "pos")
                    before = C("before")
                    pe.matmul(g[0:E, 0, 0:2], before[0:E, 0:E], cnt[0:E, :], start=True, stop=True)
                    for t in range(NT):
                        o = g[:, 1, E * t:E * (t + 1)]
                        pe.matmul(o, totbc, before[0:E, 0:E], start=True, stop=False)
                        if t:
                            pe.matmul(o, ones, oh[:, 0, :], start=False, stop=False)
                        m = pe.matmul(o, before, oh[:, t, :], start=False, stop=True)
                    m.then_inc(S["g"], 1)
                    pe.wait_ge(S["blk3"], 1)
                    g = G_use(pe, "blk")
                    pe.matmul(g[0:1, 0, 0:3 * NBLK], ones[0:E, 0:1], blk3.rearrange("p a b -> p (a b)"),
                              start=True, stop=True).then_inc(S["g"], 1)
                    pe.wait_ge(S["p01"], 1)
                    for i in range(4):
                        g = G_use(pe, ("ga", i))
                        for j in range(2):
                            for t in range(NT):
                                m = pe.matmul(g[:, j, :], hn[:, t, 2 * i + j:D:KC], onehot[:, t, :],
                                              start=(t == 0), stop=(t == NT - 1))
                        m.then_inc(S["g"], 1)
                    pe.wait_ge(S["pw"], 1)
                    for i in range(2):
                        transposes(("st", i), [weighted[:, t, P * s:P * (s + 1)] for s in (2 * i, 2 * i + 1)
                                               for t in range(NT)])

                    def products(j3, j2, parts):
                        for x, w in parts:
                            for c in range(KC):
                                m = pe.matmul(psT[:, j2, :], (x_hi, x_lo)[x][j2][:, c, :],
                                              (w_hi[j2], w_lo[j3])[w][:, :, c, :],
                                              start=(x == w == c == 0), stop=(w == 1 and c == KC - 1))
                        return m

                    def gate_up_hi(n, j3, j2):
                        pe.wait_ge(S["whi"], 2 * n)
                        pe.wait_ge(S["xh"], n)
                        products(j3, j2, [(0, 0)])
                        pe.wait_ge(S["xl"], n)
                        products(j3, j2, [(1, 0)])

                    def gate_up_lo(n, j3, j2):
                        pe.wait_ge(S["wlo"], 2 * n)
                        products(j3, j2, [(0, 1)]).then_inc(S["gu"], 1)

                    def turn_hidden(n, j2):
                        pe.wait_ge(S["hid"], n)
                        for j in range(2):
                            m = pe.transpose(psH[j2][:, BLK * j:BLK * (j + 1)], hid[:, j2, j:DE:2], ident)
                        m.then_inc(S["hid_t"], 1)

                    def down(n, j3, j2, arrived):
                        w = eslot[j3][:, 4096:6144].rearrange("p (j n) -> p j n", j=2)
                        pe.wait_ge(S[f"ed{j3}"], arrived)
                        pe.wait_ge(S["hidT"], n)
                        pe.wait_ge(S["ya"], n)
                        pe.wait_ge(S["yd"], n)
                        for k in range(8):
                            for j in range(2):
                                m = pe.matmul(psG[:, j2, k // 4, BLK * (k % 4):BLK * (k % 4 + 1)],
                                              w[:, j, P * k:P * (k + 1)], hidT[:, j2, j, :], start=(j == 0), stop=(j == 1))
                        m.then_inc(S["down"], 1)

                    G_out_upto(pe, ("ga", 3))
                    T_out_upto(pe, ("st", 1))
                    pe.wait_ge(S["pad"], 1)
                    pe.wait_ge(S["tab"], 1)
                    pe.sem_inc(S["ya"], 2)
                    pe.sem_inc(S["yd"], 2)

                    def pe_block(i, d, last=False):
                        if not last:
                            gate_up_hi(6 * i + (d + 2), (d + 1) % 3, (d + 1) % 2)
                        turn_hidden(6 * i + (d + 1), d % 2)
                        if not last:
                            gate_up_lo(6 * i + (d + 2), (d + 1) % 3, (d + 1) % 2)
                        down(6 * i + (d + 1), d % 3, d % 2, arrived(i, d))

                    gate_up_hi(1, 0, 0)
                    gate_up_lo(1, 0, 0)
                    with pe.Fori(0, N_LOOP) as i:
                        for d in range(6):
                            pe_block(i, d)
                    for d in range(N_TAIL):
                        pe_block(N_LOOP, d, d == N_TAIL - 1)
                    pe.wait_ge(S["ya"], NBLK + 2)
                    pe.wait_ge(S["yd"], NBLK + 2)
                    for s in range(4):
                        for q in range(2):
                            transposes(("y", s, q), [yT[:, n, P * s:P * (s + 1)] for n in range(4 * q, 4 * q + 4)])
                    T_out_upto(pe, ("y", 3, 1))
                    for t in range(NT):
                        g = G_use(pe, ("sc", t))
                        for n in range(2):
                            for s in range(4):
                                m = pe.matmul(g[:, n, :], stt_[:, s, t * P:(t + 1) * P], yn[:, s, 512 * n:512 * n + 512],
                                              start=(s == 0), stop=(s == 3))
                        m.then_inc(S["g"], 1)

                @block.scalar
                def _(act):
                    def T_out(name, dst, n=512, p=P, scale=1.0):
                        bank, done = T_ready(act, name)
                        act.activation(dst, bank[0:p, 0:n], ACT.Copy, scale=scale).then_inc(done, 1)

                    gate_at = [0]

                    def gate_units(n):
                        for _ in range(n):
                            if gate_at[0] == len(GATES):
                                return
                            i, t = GATES[gate_at[0]]
                            act.wait_ge(S["gate"], gate_at[0] + 1)
                            act.activation(gt[:, t, i // 2, 512 * (i % 2):512 * (i % 2) + 512], psA[:, :], ACT.Tanh,
                                           scale=0.5).then_inc(S["gate_out"], 1)
                            gate_at[0] += 1

                    T_out("pe", peT[:, :], CMP_LEN)
                    for t in range(NT):
                        act.activation(hn[:, t, :], h[:, t, :], ACT.Square, accum_out=ss[:, t:t + 1]).then_inc(S["ss"], 1)
                    act.wait_ge(S["ms"], 1)
                    act.activation(rms, rms, ACT.Sqrt).then_inc(S["rms"], 1)
                    for n in range(NZ):
                        c = min(512, D_IN - 512 * n)
                        g, done = G_ready(act, ("z", n))
                        act.activation(z[:, :, 512 * n:512 * n + c], g[:, :, 0:c], ACT.Copy).then_inc(done, 1)
                    for t in range(NT):
                        if not t:
                            G_out_upto(act, ("z", NZ - 1))
                        act.activation(kvs[:, t, 0:P], z[:, t, ZOFF["ckv"]:ZOFF["ckv"] + P], ACT.Square,
                                       accum_out=css[:, t:t + 1]).then_inc(S["ckvss"], 1)
                    act.wait_ge(S["ckvms"], 1)
                    act.activation(crms, crms, ACT.Sqrt).then_inc(S["ckvrms"], 1)
                    act.wait_ge(S["foxneg"], 1)
                    act.activation(fa, fa, ACT.Exp).then_inc(S["foxexp"], 1)
                    act.wait_ge(S["foxexp"], 1)
                    act.activation(fa, fa, ACT.Ln, bias=1.0).then_inc(S["foxln"], 1)
                    act.activation(ga, z[:, :, ZOFF["g_a"]:ZOFF["g_a"] + 12].rearrange("p t (h g) -> p t h g", h=H),
                                   ACT.Tanh, scale=0.5).then_inc(S["foxln"], 1)
                    gate_units(2)
                    for i in range(2):
                        T_out(("src", i), tr[:, 2 * i:2 * i + 2, :].rearrange("p n t -> p (n t)"))
                    g, done = G_ready(act, "cum")
                    act.activation(cumb[:, 0, :].rearrange("p (a b) -> p a b", a=2), g[0:H, :, 0:P], ACT.Copy)
                    act.activation(cumb[:, 1, :].rearrange("p (a b) -> p a b", a=2), g[0:H, :, 0:P], ACT.Copy,
                                   scale=-1.0).then_inc(done, 1)
                    gate_units(1)
                    for i in range(2, 4):
                        T_out(("src", i), tr[:, 2 * i:2 * i + 2, :].rearrange("p n t -> p (n t)"))
                    for t in range(NT):
                        w = P * (t + 1)
                        g, done = G_ready(act, ("idx", t))
                        act.activation(sm[t][:, :, 0:w], g.rearrange("p a (b s) -> p (a b) s", b=2)[:, :, 0:w],
                                       ACT.Relu, scale=SCALE).then_inc(done, 1)
                    act.wait_ge(S["small2"], 16 * 8)
                    bank, done = T_ready(act, "ckv")
                    act.activation(tr[:, TSLOT["ckv"], :], bank[:, 0:T], ACT.Copy, scale=ckvg[:, 0:1]).then_inc(done, 1)
                    gate_units(1)
                    g, done = G_ready(act, "kvc")
                    act.activation(kvs[:, :, :], g, ACT.Copy).then_inc(done, 1)
                    for i in range(4, 9):
                        T_out(("src", i), tr[:, 2 * i:2 * i + 2, :].rearrange("p n t -> p (n t)"))
                    T_out("kc", tr[:, 20:22, :].rearrange("p n t -> p (n t)"))
                    g, done = G_ready(act, "cmph")
                    act.activation(gx.rearrange("p (a b) -> p a b", a=2), g[0:N_CMP, :, 0:CMP_HID], ACT.Copy)
                    act.activation(gb.rearrange("p (a b) -> p a b", a=2), g[0:N_CMP, :, 0:CMP_HID], ACT.Square)\
                        .then_inc(done, 1)
                    act.wait_ge(S["gelu_b"], 1)
                    act.activation(gb, gb, ACT.Tanh, scale=GELU_C).then_inc(S["gelu_th"], 1)
                    gate_units(2)
                    bank, done = T_ready(act, "cmph")
                    act.activation(hcT.rearrange("p j c -> p (j c)"), bank[:, 0:4 * N_CMP], ACT.Copy, scale=0.5)\
                        .then_inc(done, 1)
                    g, done = G_ready(act, "cmpo")
                    act.activation(kcT, g[:, 0, 0:N_CMP], ACT.Copy)
                    act.activation(vcs[:, :], g[0:N_CMP, 1, 0:DH], ACT.Copy).then_inc(done, 1)

                    NU = len(UNITS)
                    for u, (m_, t) in enumerate(UNITS):
                        w = N_CMP if m_ == "cmp" else P * (t + 1)
                        act.wait_ge(S["sm"], u + 1)
                        for x in range(H):
                            act.activation(sm[u % 2][:, x, 0:w], sm[u % 2][:, x, 0:w], ACT.Exp, bias=nmx[:, u, x:x + 1],
                                           accum_out=ssum[:, u, x:x + 1]).then_inc(S["exp"], 1)
                        if m_ == "swa":
                            act.wait_ge(S["sink"], t + 1)
                            act.activation(ssum[:, 12 + t, :], nmx[:, 12 + t, :], ACT.Exp).then_inc(S["sinkexp"], 1)
                        gate_units(1)
                        kt = NT if t and m_ != "cmp" else 1
                        wp = N_CMP if m_ == "cmp" else P
                        if u:
                            act.wait_ge(S["pv"], u)
                        for i in range(kt):
                            T_out(("p", u, i), ptb[0:wp, 512 * i:512 * (i + 1)], 512, wp)
                    gate_units(16)
                    for i in range(4):
                        T_out(("o", i), oT[:, i].rearrange("p c t -> p (c t)"))
                    for t in range(NT):
                        for q in range(2):
                            T_out(("m", t, q), hnT[:, 4 * q:4 * q + 4, t * P:(t + 1) * P], scale=0.5)
                    for t in range(NT):
                        act.wait_ge(S["h"], t + 1)
                        act.activation(hn[:, t, :], h[:, t, :], ACT.Square, accum_out=ss[:, t:t + 1]).then_inc(S["ss2"], 1)
                    act.wait_ge(S["ms2"], 1)
                    act.activation(rms, rms, ACT.Sqrt).then_inc(S["rms2"], 1)
                    act.wait_ge(S["gexp_in"], 1)
                    act.activation(g8b, g8b, ACT.Exp).then_inc(S["gexp"], 1)
                    act.wait_ge(S["texp_in"], 1)
                    act.activation(ee, ee, ACT.Exp).then_inc(S["texp"], 1)
                    for i in range(4):
                        g, done = G_ready(act, ("ga", i))
                        act.activation(xs[:, 2 * i, 0:PAIRS], g[:, 0, :], ACT.Copy, scale=gain2[:, 2 * i:2 * i + 1])
                        act.activation(xs[:, 2 * i + 1, 0:PAIRS], g[:, 1, :], ACT.Copy,
                                       scale=gain2[:, 2 * i + 1:2 * i + 2]).then_inc(done, 1)
                    for i in range(2):
                        T_out(("st", i), stt_[:, 2 * i:2 * i + 2, :].rearrange("p s t -> p (s t)"))

                    def round_block(b, n, j3, j2, arrived):
                        c = act.value_load(tab[0:1, 1, bass.ds(b, 1)], min_val=0, max_val=PAIRS)
                        act.activation(x_hi[j2][:, :, :], xs[:, :, bass.ds(c, BLK)], ACT.Copy).then_inc(S["xh"], 1)
                        for k, name in enumerate("gu"):
                            act.wait_ge(S[f"e{name}{j3}"], arrived)
                            act.activation(w_hi[j2][:, k], eslot[j3][:, 2048 * k:2048 * (k + 1)].rearrange(
                                "p (k n) -> p k n", k=KC), ACT.Copy).then_inc(S["whi"], 1)

                    def tanh_gate(n, j2):
                        act.wait_ge(S["gu"], n)
                        act.activation(th[:, j2], psT[:, j2, 0:DE], ACT.Tanh, scale=0.5).then_inc(S["th"], 1)

                    def hidden_out(n, j2):
                        act.wait_ge(S["hid_t"], n)
                        act.activation(hidT[:, j2], psH[j2].rearrange("p (j s) -> p j s", j=2), ACT.Copy)\
                            .then_inc(S["hidT"], 1)

                    def y_out(n, b, j2):
                        c = act.value_load(tab[0:1, 1, bass.ds(b, 1)], min_val=0, max_val=PAIRS)
                        act.wait_ge(S["down"], n)
                        act.wait_ge(S["ya"], n + 1)
                        act.activation(yT[:, 0:4, bass.ds(c, BLK)], psG[:, j2, 0, :].rearrange("p (n s) -> p n s", n=4),
                                       ACT.Copy).then_inc(S["ya"], 1)

                    act.wait_ge(S["tab"], 1)
                    act.wait_ge(S["pad"], 1)
                    T_out_upto(act, ("st", 1))
                    G_out_upto(act, ("ga", 3))
                    round_block(0, 1, 0, 0, 16)
                    round_block(1, 2, 1, 1, 16)
                    tanh_gate(1, 0)
                    def act_block(i, d, ahead=2):
                        hidden_out(6 * i + (d + 1), d % 2)
                        if ahead == 2:
                            round_block(6 * i + (d + 2), 6 * i + (d + 3), (d + 2) % 3, d % 2, arrived(i, d + 2))
                        if ahead:
                            tanh_gate(6 * i + (d + 2), (d + 1) % 2)
                        y_out(6 * i + (d + 1), 6 * i + d, d % 2)

                    with act.Fori(0, N_LOOP) as i:
                        for d in range(6):
                            act_block(i, d)
                    for d in range(N_TAIL):
                        act_block(N_LOOP, d, min(2, N_TAIL - 1 - d))
                    for s in range(4):
                        T_out(("y", s, 0), yn[:, s, 0:512])

                @block.gpsimd
                def _(pool):
                    for i, name in enumerate(TWINS):
                        c = SRC[name][0]
                        pool.wait_ge(S["rope"], {"ki": 1, "ksel": 3, "kwin": 3}.get(name, 5))
                        pool.tensor_copy(twin[:, :, i, :].rearrange("p t (a d) -> p t a d", a=2),
                                         z[:, :, c:c + DH].unsqueeze(2).broadcast_to([P, NT, 2, DH])).then_inc(S["twin"], 1)

                @block.vector
                def _(dve):
                    n_link = [0]

                    def link(ins):
                        n_link[0] += 1
                        ins.then_inc(S["dve"], 1)
                        dve.wait_ge(S["dve"], n_link[0])

                    TT, TS, STT = dve.tensor_tensor, dve.tensor_scalar, dve.scalar_tensor_tensor

                    dve.wait_ge(S["small"], 16 * 7)
                    g, done = G_ready(dve, "bc")
                    dve.tensor_copy(bc[:, :], g[:, 0, 0:80]).then_inc(done, 1)
                    dve.wait_ge(done, 1)
                    dve.wait_ge(S["ss"], NT)
                    TS(rms, ss, 1.0 / D, EPS, ALU.mult, ALU.add).then_inc(S["ms"], 1)
                    dve.wait_ge(S["rms"], 1)
                    link(dve.reciprocal(rstd, rms))
                    for t in range(NT):
                        TS(hn[:, t, :], h[:, t, :], rstd[:, t:t + 1], None, ALU.mult).then_inc(S["hn"], 1)

                    def hnT_out(kind, gain):
                        for t in range(NT):
                            for q in range(2):
                                bank, done = T_ready(dve, (kind, t, q))
                                TT(hnT[:, 4 * q:4 * q + 4, t * P:(t + 1) * P], bank.rearrange("p (k t) -> p k t", k=4),
                                   gain[:, 4 * q:4 * q + 4].unsqueeze(2).broadcast_to([P, 4, P]), ALU.mult
                                   ).then_inc(S["hnt"], 1)
                                fence(done)

                    n_h = [0]

                    def fence(done):
                        n_h[0] += 1
                        dve.wait_ge(S["hnt"], n_h[0])
                        dve.sem_inc(done, 1)

                    hnT_out("hn", gain1)
                    G_out_upto(dve, ("z", NZ - 1))
                    link(TT(fx, z[:, :, ZOFF["f_b"]:ZOFF["f_b"] + H],
                            bc[:, 72:76].unsqueeze(1).broadcast_to([P, NT, H]), ALU.add))
                    link(TS(fa, fx, -1.0, None, ALU.mult))
                    TT(fa, fa, fx, ALU.min).then_inc(S["foxneg"], 1)
                    dve.wait_ge(S["ckvss"], NT)
                    TS(crms, css, 1.0 / P, EPS, ALU.mult, ALU.add).then_inc(S["ckvms"], 1)

                    def rope(x, n, tmps):
                        c = cos[:, :, :].unsqueeze(2).broadcast_to([P, NT, n, DH])
                        s = sin[:, :, :].unsqueeze(2).broadcast_to([P, NT, n, DH])
                        a, b = (v[:, 0:NT * n * DH].rearrange("p (t n d) -> p t n d", t=NT, n=n) for v in tmps)
                        TT(a, x, c, ALU.mult)
                        TT(b[:, :, :, 0:32], x[:, :, :, 32:64], s[:, :, :, 0:32], ALU.mult)
                        link(TT(b[:, :, :, 32:64], x[:, :, :, 0:32], s[:, :, :, 32:64], ALU.mult))
                        return TT(x, a, b, ALU.add)

                    def rope_group(i):
                        c, n, step = ROPE[i]
                        x = z[:, :, c:c + n * step].rearrange("p t (n s) -> p t n s", s=step)[:, :, :, 0:DH] \
                            if step != DH else z[:, :, c:c + n * DH].rearrange("p t (n s) -> p t n s", s=DH)
                        m = rope(x, n, [oall[:, t].rearrange("p i w -> p (i w)") for t in range(NT)])
                        m.then_inc(S["rope"], 1)
                        n_rope[0] += 1
                        dve.wait_ge(S["rope"], n_rope[0])

                    n_rope = [0]
                    dve.wait_ge(S["hnt"], 4)
                    rope_group(3)
                    dve.wait_ge(S["foxln"], 2)
                    link(TS(fx, fx, 0.0, None, ALU.min))
                    TT(logf, fx, fa, ALU.subtract).then_inc(S["logf"], 1)
                    rope_group(1)
                    link(TS(wi, z[:, :, ZOFF["w_i"]:ZOFF["w_i"] + H], 0.5, None, ALU.mult))
                    rope_group(0)
                    dve.wait_ge(S["ckvrms"], 1)
                    link(dve.reciprocal(crstd, crms))
                    for t in range(NT):
                        m = TS(kvs[:, t, 0:P], z[:, t, ZOFF["ckv"]:ZOFF["ckv"] + P], crstd[:, t:t + 1], None, ALU.mult)
                    m.then_inc(S["ckvn"], 1)
                    rope_group(2)
                    rope_group(4)
                    link(TS(ga, ga, 0.5, 0.5, ALU.mult, ALU.add))
                    i = T_AT[("src", 3)]
                    dve.wait_ge(S[f"te{i % 2}"], i // 2 + 1)
                    dve.wait_ge(S[f"te{T_AT['pe'] % 2}"], 1)
                    for a in range(2):
                        m = TT(zc[:, 16 * a:16 * a + 16, :],
                               tr[:, TSLOT["kvcmp"], 16 * a:16 * a + 16 * N_CMP].rearrange("p (c r) -> p r c", r=16),
                               peT[:, 16 * a:16 * a + 16].unsqueeze(2).broadcast_to([P, 16, N_CMP]), ALU.add)
                    m.then_inc(S["zc"], 1)
                    for t in range(NT):
                        w = P * (t + 1)
                        i = G_AT[("idx", t)]
                        dve.wait_ge(S[f"ge{i % 2}"], i // 2 + 1)
                        link(TS(sel[:, t, 0:w], sm[t][:, AT[0], 0:w], wi[:, t, 0:1], None, ALU.mult))
                        for x in range(1, H):
                            link(STT(out=sel[:, t, 0:w], in0=sm[t][:, AT[x], 0:w], scalar=wi[:, t, x:x + 1],
                                     in1=sel[:, t, 0:w], op0=ALU.mult, op1=ALU.add))
                        link(TT(sel[:, t, 0:w], sel[:, t, 0:w], causal[t], ALU.add))
                    i = G_AT["kvc"]
                    dve.wait_ge(S[f"ge{i % 2}"], i // 2 + 1)
                    m = rope(kvs[:, :, 0:W].rearrange("p t (n s) -> p t n s", s=DH), H,
                             [ptb[:, 0:512], ptb[:, 512:1024]])
                    m.then_inc(S["kvrope"], 1)
                    i = G_AT["cmph"]
                    dve.wait_ge(S[f"ge{i % 2}"], i // 2 + 1)
                    link(TS(gb, gb, 0.044715, 1.0, ALU.mult, ALU.add))
                    TT(gb, gb, gx, ALU.mult).then_inc(S["gelu_b"], 1)
                    dve.wait_ge(S["gelu_th"], 1)
                    STT(out=gx, in0=gb, scalar=1.0, in1=gx, op0=ALU.add, op1=ALU.mult).then_inc(S["gelu"], 1)

                    def topk(t):
                        w = P * (t + 1)
                        a = sel[:, t, 0:w]
                        for _ in range(TOPK // 8):
                            link(dve.max(m8, a))
                            link(dve.match_replace(a, m8, a, TAKEN))
                        link(TS(a, a, TAKEN, -1.0, ALU.is_equal, ALU.add))
                        link(STT(out=a, in0=a, scalar=-NEG, in1=causal[t], op0=ALU.mult, op1=ALU.add))

                    sinks = bc[:, 76:80].rearrange("p (b a) -> p b a", b=2)

                    def softmax_in(u):
                        m_, t = UNITS[u]
                        w = N_CMP if m_ == "cmp" else P * (t + 1)
                        mask = {"cmp": cmp_mask, "swa": swa_mask, "dsa": [sel[:, i, 0:P * (i + 1)] for i in range(NT)]
                                }.get(m_, causal)[t]
                        g, done = G_ready(dve, ("s", u))
                        if u >= 2:
                            dve.wait_ge(S["pv"], u - 1)
                        s = sm[u % 2][:, :, 0:w]
                        STT(out=s, in0=g.rearrange("p a (b s) -> p (a b) s", b=2)[:, :, 0:w], scalar=SCALE,
                            in1=mask.unsqueeze(1).broadcast_to([P, H, w]), op0=ALU.mult, op1=ALU.add).then_inc(done, 1)
                        i = G_AT[("s", u)]
                        dve.wait_ge(done, i // 2 + 1)
                        if m_ == "swa":
                            link(dve.reduce_max(nmx[:, u, :], s, AXX))
                            link(TT(by_head(nmx[:, u, :]), by_head(nmx[:, u, :]), sinks, ALU.max))
                            link(TS(nmx[:, u, :], nmx[:, u, :], -1.0, None, ALU.mult))
                            TT(by_head(nmx[:, 12 + t, :]), by_head(nmx[:, u, :]), sinks, ALU.add).then_inc(S["sink"], 1)
                            dve.wait_ge(S["sink"], t + 1)
                            dve.sem_inc(S["sm"], 1)
                        else:
                            dve.reduce_max(nmx[:, u, :], s, AXX, negate=True).then_inc(S["sm"], 1)

                    def combine(u):
                        m_, t = UNITS[u]
                        dve.wait_ge(S["exp"], H * (u + 1))
                        if m_ == "swa":
                            dve.wait_ge(S["sinkexp"], t + 1)
                            link(TT(ssum[:, u, :], ssum[:, u, :], ssum[:, 12 + t, :], ALU.add))
                        link(dve.reciprocal(coef, ssum[:, u, :]))
                        if m_ in GATE_OF:
                            link(TT(by_head(coef), by_head(coef),
                                    ga[:, t, :, GATE_OF[m_]].rearrange("p (b a) -> p b a", b=2), ALU.mult))
                        if m_ == "cmp":
                            link(TS(coef, coef, C("cmp_row")[:, t:t + 1], None, ALU.mult))
                        dve.wait_ge(S["pv"], u + 1)
                        o = oall[:, t, OUT_OF[m_], :].rearrange("p (h d) -> p h d", h=H)
                        add = m_ in ("win", "cmp")
                        dst = otmp[:, :].rearrange("p (h d) -> p h d", h=H) if add else o
                        m = TT(dst.rearrange("p (b a) d -> p b a d", b=2),
                               psO[:, u % 2, :].rearrange("p (b a d) -> p b a d", b=2, a=2),
                               by_head(coef).unsqueeze(3).broadcast_to([P, 2, 2, DH]), ALU.mult)
                        if add:
                            link(m)
                            m = TT(o, o, dst, ALU.add)
                        m.then_inc(S["oc"], 1)
                        dve.wait_ge(S["oc"], u + 1)

                    NU = len(UNITS)
                    softmax_in(0)
                    for u in range(NU):
                        if u == 2:
                            topk(0)
                        if u == 5:
                            topk(1)
                        if u + 1 < NU:
                            softmax_in(u + 1)
                        combine(u)
                    dve.wait_ge(S["gate_out"], len(GATES))
                    for t in range(NT):
                        for n in range(2):
                            for i2 in range(2):
                                g, done = G_ready(dve, ("mg", t, n, i2))
                                o = merged[:, t, 512 * n:512 * n + 512]
                                for j in range(2):
                                    first = not i2 and not j
                                    m = STT(out=o if first else mtmp, in0=gt[:, t, 2 * i2 + j, 512 * n:512 * n + 512],
                                            scalar=1.0, in1=g[:, j, :], op0=ALU.add, op1=ALU.mult)
                                    link(m)
                                    if not first:
                                        m = TT(o, o, mtmp, ALU.add)
                                        if j:
                                            m.then_inc(done, 1)
                                            dve.wait_ge(done, G_AT[("mg", t, n, i2)] // 2 + 1)
                                        else:
                                            link(m)
                    for t in range(NT):
                        g, done = G_ready(dve, ("wo", t))
                        TT(h[:, t, :], h[:, t, :], g.rearrange("p a n -> p (a n)"), ALU.add).then_inc(done, 1)
                        dve.wait_ge(done, G_AT[("wo", t)] // 2 + 1)
                        dve.sem_inc(S["h"], 1)
                    dve.wait_ge(S["ss2"], NT)
                    TS(rms, ss, 1.0 / D, EPS, ALU.mult, ALU.add).then_inc(S["ms2"], 1)
                    dve.wait_ge(S["rms2"], 1)
                    link(dve.reciprocal(rstd, rms))
                    for t in range(NT):
                        TS(hn[:, t, :], h[:, t, :], rstd[:, t:t + 1], None, ALU.mult).then_inc(S["hn2"], 1)
                    dve.memset(xs[:, :, PAIRS:SLOTS], 0.0).then_inc(S["pad"], 1)
                    dve.wait_ge(S["small2"], 16 * 8)
                    hnT_out("hn2", gain2)

                    g, done = G_ready(dve, "router")
                    dve.tensor_copy(lg, g[:, :, 0:GROUPS + E]).then_inc(done, 1)
                    dve.wait_ge(done, G_AT["router"] // 2 + 1)
                    gl, el = lg[:, :, 0:GROUPS], lg[:, :, GROUPS:]

                    def first_max(x, n, v, oh_, tmp, rank):
                        link(dve.reduce_max(v, x, AXX))
                        link(TT(tmp, x, v.unsqueeze(2).broadcast_to([P, NT, n]), ALU.is_equal))
                        link(TT(tmp, tmp, rank.unsqueeze(1).broadcast_to([P, NT, n]), ALU.mult))
                        link(dve.reduce_max(ee, tmp, AXX))
                        link(TT(oh_, tmp, ee.unsqueeze(2).broadcast_to([P, NT, n]), ALU.is_equal))

                    first_max(gl, GROUPS, gmx, ohg, g8, C("rank8"))
                    TT(g8b, gl, gmx.unsqueeze(2).broadcast_to([P, NT, GROUPS]), ALU.subtract).then_inc(S["gexp_in"], 1)
                    link(TS(g8, ohg, 1.0, -NEG, ALU.subtract, ALU.mult))
                    link(TT(em.rearrange("p t (g e) -> p t g e", g=GROUPS), el.rearrange("p t (g e) -> p t g e", g=GROUPS),
                            g8.unsqueeze(3).broadcast_to([P, NT, GROUPS, PER_GROUP]), ALU.add))
                    first_max(em, E, v1, oh1, eq, C("rank64"))
                    link(STT(out=em, in0=oh1, scalar=NEG, in1=em, op0=ALU.mult, op1=ALU.add))
                    first_max(em, E, v2, oh2, eq, C("rank64"))
                    TT(oh, oh1, oh2, ALU.add).then_inc(S["oh"], 1)
                    TT(ee, v2, v1, ALU.subtract).then_inc(S["texp_in"], 1)
                    dve.wait_ge(S["gexp"], 1)
                    link(dve.reduce_sum(pg, g8b, AXX))
                    link(dve.reciprocal(pg, pg))
                    g, done = G_ready(dve, "tot")
                    link(dve.tensor_copy(cnt[0:E, 0:1], g[0:E, 0, 0:1]))
                    link(TS(cnt[0:E, 1:2], cnt[0:E, 0:1], 0.5, None, ALU.is_gt))
                    link(STT(out=cnt[0:E, 1:2], in0=cnt[0:E, 0:1], scalar=BLK + 0.5, in1=cnt[0:E, 1:2],
                             op0=ALU.is_gt, op1=ALU.add))
                    TS(totbc, ones[0:E, :], cnt[0:E, 0:1], None, ALU.mult).then_inc(done, 1)
                    dve.wait_ge(done, G_AT["tot"] // 2 + 1)
                    dve.sem_inc(S["cnt"], 1)
                    dve.wait_ge(S["texp"], 1)
                    link(TS(w1s, ee, 1.0, None, ALU.add))
                    link(dve.reciprocal(w1s, w1s))
                    link(TT(w1s, w1s, pg, ALU.mult))
                    link(TT(w2s, w1s, ee, ALU.mult))
                    g, done = G_ready(dve, "pos")
                    link(dve.tensor_copy(pos[0:E, :], g[0:E, 0, 0:2]))
                    place = g[:, 1, 0:NT * E].rearrange("p (t e) -> p t e", t=NT)
                    link(TT(eq, oh1, place, ALU.mult))
                    link(dve.reduce_sum(d1, eq, AXX))
                    link(TT(eq, oh2, place, ALU.mult))
                    dve.reduce_sum(d2, eq, AXX).then_inc(done, 1)
                    dve.wait_ge(done, G_AT["pos"] // 2 + 1)
                    blkn = C("block")[0:E, :]
                    link(TT(bend[0:E], pos[0:E, 1:2], cnt[0:E, 1:2], ALU.add))
                    link(TS(c0[0:E], pos[0:E, 1:2], -float(BLK), None, ALU.mult))
                    link(TT(c0[0:E], c0[0:E], pos[0:E, 0:1], ALU.add))
                    link(TS(blk3[:, 1, :], blkn, pos[0:E, 1:2], None, ALU.is_ge))
                    link(STT(out=blk3[:, 2, :], in0=blkn, scalar=bend[0:E], in1=blk3[:, 1, :], op0=ALU.is_lt,
                             op1=ALU.mult))
                    link(TS(blk3[:, 0, :], blkn, float(BLK), c0[0:E], ALU.mult, ALU.add))
                    link(TT(blk3[:, 0, :], blk3[:, 0, :], blk3[:, 2, :], ALU.mult))
                    TS(blk3[:, 1, :], blk3[:, 2, :], C("expert")[0:E], None, ALU.mult).then_inc(S["blk3"], 1)
                    slots = C("slot")
                    for t in range(NT):
                        link(TS(onehot[:, t, :], slots, d1[:, t:t + 1], None, ALU.is_equal))
                        link(STT(out=onehot[:, t, :], in0=slots, scalar=d2[:, t:t + 1], in1=onehot[:, t, :],
                                 op0=ALU.is_equal, op1=ALU.add))
                    dve.sem_inc(S["p01"], 1)
                    g, done = G_ready(dve, "blk")
                    b3 = g[0:1, 0, 0:3 * NBLK].rearrange("p (a b) -> p a b", a=3)
                    link(TS(tabf[:, 0, :], b3[:, 2, :], -1.0, 1.0, ALU.mult, ALU.add))
                    link(STT(out=tab[:, 1, :], in0=tabf[:, 0, :], scalar=float(PAIRS), in1=b3[:, 0, :],
                             op0=ALU.mult, op1=ALU.add))
                    STT(out=tab[:, 0, :], in0=tabf[:, 0, :], scalar=float(E - 1), in1=b3[:, 1, :],
                        op0=ALU.mult, op1=ALU.add).then_inc(done, 1)
                    dve.wait_ge(done, G_AT["blk"] // 2 + 1)
                    dve.sem_inc(S["tab"], 1)
                    for t in range(NT):
                        link(TS(weighted[:, t, :], slots, d1[:, t:t + 1], w1s[:, t:t + 1], ALU.is_equal, ALU.mult))
                        link(TS(mtmp, slots, d2[:, t:t + 1], w2s[:, t:t + 1], ALU.is_equal, ALU.mult))
                        link(TT(weighted[:, t, :], weighted[:, t, :], mtmp, ALU.add))
                    dve.sem_inc(S["pw"], 1)

                    def rest_of_block(b, n, j3, j2):
                        c = dve.value_load(tab[0:1, 1, bass.ds(b, 1)], min_val=0, max_val=PAIRS)
                        dve.wait_ge(S["xh"], n)
                        TT(x_lo[j2][:, :, :], xs[:, :, bass.ds(c, BLK)], x_hi[j2][:, :, :].bitcast(F32), ALU.subtract)\
                            .then_inc(S["xl"], 1)
                        for k in range(2):
                            dve.wait_ge(S["whi"], 2 * n + (k - 1))
                            w = eslot[j3][:, 2048 * k:2048 * (k + 1)].rearrange("p (k n) -> p k n", k=KC)
                            TT(w_lo[j3][:, k], w, w_hi[j2][:, k].bitcast(F32), ALU.subtract).then_inc(S["wlo"], 1)

                    def swiglu(n, j2):
                        dve.wait_ge(S["th"], n)
                        STT(out=hida[:, j2], in0=th[:, j2], scalar=1.0, in1=psT[:, j2, 0:DE], op0=ALU.add, op1=ALU.mult)\
                            .then_inc(S["hid_a"], 1)
                        dve.wait_ge(S["hid_a"], n)
                        STT(out=hid[:, j2], in0=hida[:, j2], scalar=0.5, in1=psT[:, j2, DE:2 * DE], op0=ALU.mult,
                            op1=ALU.mult).then_inc(S["hid"], 1)

                    def y_out(n, b, j2):
                        c = dve.value_load(tab[0:1, 1, bass.ds(b, 1)], min_val=0, max_val=PAIRS)
                        dve.wait_ge(S["down"], n)
                        dve.wait_ge(S["yd"], n + 1)
                        dve.tensor_copy(yT[:, 4:8, bass.ds(c, BLK)], psG[:, j2, 1, :].rearrange("p (n s) -> p n s", n=4))\
                            .then_inc(S["yd"], 1)

                    def dve_block(i, d, ahead=2):
                        if ahead == 2:
                            rest_of_block(6 * i + (d + 2), 6 * i + (d + 3), (d + 2) % 3, d % 2)
                        if ahead:
                            swiglu(6 * i + (d + 2), (d + 1) % 2)
                        y_out(6 * i + (d + 1), 6 * i + d, d % 2)

                    rest_of_block(0, 1, 0, 0)
                    rest_of_block(1, 2, 1, 1)
                    swiglu(1, 0)
                    with dve.Fori(0, N_LOOP) as i:
                        for d in range(6):
                            dve_block(i, d)
                    for d in range(N_TAIL):
                        dve_block(N_LOOP, d, min(2, N_TAIL - 1 - d))
                    for s in range(4):
                        bank, done = T_ready(dve, ("y", s, 1))
                        dve.tensor_copy(yn[:, s, 512:1024], bank).then_inc(done, 1)
                    for t in range(NT):
                        g, done = G_ready(dve, ("sc", t))
                        link(TT(h[:, t, :], h[:, t, :], g.rearrange("p a n -> p (a n)"), ALU.add))

            nc.all_engine_barrier()
            for n in ALL_SEMS:
                nc.sync.sem_clear(S[n])
            nc.all_engine_barrier()

        with nc.Block() as block:
            @block.tensor
            def _(pe):
                pe.wait_ge(s_pre["dma"], 80)
                for n in range(2):
                    m = pe.matmul(psG[:, 0, n, :], ones[0:1, :], fin[0:1, 512 * n:512 * n + 512], start=True, stop=True)
                m.then_inc(s_pre["g"], 1)

            @block.scalar
            def _(act):
                for t in range(NT):
                    act.activation(hn[:, t, :], h[:, t, :], ACT.Square, accum_out=ss[:, t:t + 1]).then_inc(s_pre["ss"], 1)
                act.wait_ge(s_pre["ms"], 1)
                act.activation(rms, rms, ACT.Sqrt).then_inc(s_pre["rms"], 1)

            @block.vector
            def _(dve):
                dve.wait_ge(s_pre["ss"], NT)
                dve.tensor_scalar(rms, ss, 1.0 / D, EPS, ALU.mult, ALU.add).then_inc(s_pre["ms"], 1)
                dve.wait_ge(s_pre["rms"], 1)
                dve.reciprocal(rstd, rms).then_inc(s_pre["fin"], 1)
                dve.wait_ge(s_pre["fin"], 1)
                dve.wait_ge(s_pre["g"], 1)
                for t in range(NT):
                    dve.scalar_tensor_tensor(out=hn[:, t, :], in0=h[:, t, :], scalar=rstd[:, t:t + 1],
                                             in1=psG[:, 0].rearrange("p a n -> p (a n)"), op0=ALU.mult, op1=ALU.mult
                                             ).then_inc(s_pre["y"], 1)

            @block.sync
            def _(sp):
                sp.dma_start(fin, A["final_norm"].rearrange("(a d) -> a d", a=1)).then_inc(s_pre["dma"], 16)
                for t in range(NT):
                    sp.wait_ge(s_pre["y"], t + 1)
                    sp.dma_start(out[0, t * P:(t + 1) * P, :], hn[:, t, :]).then_inc(s_pre["out"], 16)
                sp.wait_ge(s_pre["out"], 16 * NT)


_INS = ["x", "positions", "attn_norm", "w_in", "nsa_pe_k", "nsa_w1_k", "nsa_w2_k", "nsa_pe_v", "nsa_w1_v", "nsa_w2_v",
        "fox_forget_bias", "dsa_kv_norm", "dsa_w_ukv", "swa_sinks", "w_branch", "w_gate", "w_out", "ffn_norm",
        "moe_w_group", "moe_b_group", "moe_w_expert", "moe_b_expert", "moe_w_gate", "moe_w_up", "moe_w_down",
        "final_norm"]


def kernel(**inputs):
    import concourse.bacc as _bacc
    from concourse.bass_utils import run_bass_kernel_spmd as _run

    nc = _bacc.Bacc("TRN2", target_bir_lowering=False, num_devices=1)
    arrays = {name: np.ascontiguousarray(inputs[name]) for name in _INS}
    arrays["consts"] = constants()
    args = {name: nc.dram_tensor(f"in_{name}", a.shape, mybir.dt.from_np(a.dtype), kind="ExternalInput").ap()
            for name, a in arrays.items()}
    out = nc.dram_tensor("out_0", (1, T, D), F32, kind="ExternalOutput").ap()
    trunk(nc, args, out)
    r = _run(nc, [{f"in_{name}": a for name, a in arrays.items()}], core_ids=[0])
    return r.results[0]["out_0"]
```

```python
from contextlib import ExitStack, nullcontext

import numpy as np

import concourse.bass as bass
from concourse import mybir

F32 = mybir.dt.float32
F32R = mybir.dt.float32r
I32 = mybir.dt.int32
ALU = mybir.AluOpType
ACT = mybir.ActivationFunctionType
AXX = mybir.AxisListType.X

P = 128
D = 1024
T = 256
NT = T // P
KC = D // P
DEPTH = 2
DH = 64
H = 4
W = H * DH
CMP_LEN, CMP_STRIDE, CMP_HID = 32, 16, 256
N_CMP = (T - CMP_LEN) // CMP_STRIDE + 1
TOPK = T // 4
SWA_WIN = 128
GROUPS, PER_GROUP = 8, 8
E = GROUPS * PER_GROUP
DE = 256
PAIRS = 2 * T
BLK = 128
NBLK = E + (PAIRS - E) // BLK
N_LOOP = (NBLK - 2) // 6
N_TAIL = NBLK - 6 * N_LOOP
SLOTS = PAIRS + BLK
NEG = -1e30
TAKEN = float(np.float32(-3e38))
EPS = 1e-6
SCALE = DH ** -0.5
GELU_C = 0.7978845608028654

ZOFF, _o = {}, 0
for _n, _w in (("q_a", W), ("k_cmp", DH), ("v_cmp", DH), ("k_sel", DH), ("v_sel", DH), ("k_win", DH),
               ("v_win", DH), ("g_a", H * 3), ("q_b", W), ("k_b", W), ("v_b", W), ("f_b", H), ("q_c", W),
               ("ckv", P), ("q_i", W), ("k_i", DH), ("w_i", H), ("q_d", W), ("k_d", 2 * DH), ("v_d", 2 * DH)):
    ZOFF[_n] = _o
    _o += _w
D_IN = _o
NZ = -(-D_IN // 512)

CONST = {}
_c = 0
for _n, _w in (("ident", P), ("causal", T), ("swa", T), ("cmp", NT * N_CMP), ("cmp_row", NT), ("before", P),
               ("upto", P), ("ones", P), ("inv_freq", 32), ("slot", PAIRS), ("block", NBLK), ("expert", 1),
               ("eye8", H), ("rank8", GROUPS), ("rank64", E)):
    CONST[_n] = (_c, _w)
    _c += _w
N_CONST = _c


def constants():
    c = np.zeros((P, N_CONST), np.float32)

    def put(name, v):
        o, w = CONST[name]
        c[:, o:o + w] = np.asarray(v, np.float32).reshape(P, w)

    p = np.arange(P)[:, None]
    put("ident", np.eye(P))
    t = p[:, :, None] + P * np.arange(NT)[None, :, None]
    s = np.arange(T)[None, None, :]
    last = t[:, 1:2]
    put("causal", np.where(s <= last, 0.0, NEG))
    put("swa", np.where((s <= last) & (last - s < SWA_WIN), 0.0, NEG))
    seen = CMP_STRIDE * np.arange(N_CMP)[None, None, :] + CMP_LEN - 1 <= t
    put("cmp", np.where(seen, 0.0, NEG))
    put("cmp_row", seen.any(-1))
    put("before", p < np.arange(P)[None])
    put("upto", p <= np.arange(P)[None])
    put("ones", np.ones((P, P)))
    put("inv_freq", np.broadcast_to(10000.0 ** (-np.arange(32) / 32.0), (P, 32)))
    put("slot", np.broadcast_to(np.arange(PAIRS), (P, PAIRS)))
    put("block", np.broadcast_to(np.arange(NBLK), (P, NBLK)))
    put("expert", p)
    put("eye8", 8.0 * np.eye(P)[:, :H])
    put("rank8", np.broadcast_to(GROUPS - np.arange(GROUPS), (P, GROUPS)))
    put("rank64", np.broadcast_to(E - np.arange(E), (P, E)))
    return c


ROPE = [(ZOFF["k_sel"], 2, 2 * DH), (ZOFF["q_a"], 5, DH), (ZOFF["q_c"], 4, DH), (ZOFF["q_i"], 5, DH),
        (ZOFF["q_d"], 6, DH)]
SRC = {"qb0": (ZOFF["q_b"], 0), "qb1": (ZOFF["q_b"] + P, 0), "kb0": (ZOFF["k_b"], 0), "kb1": (ZOFF["k_b"] + P, 0),
       "qi0": (ZOFF["q_i"], 0), "qi1": (ZOFF["q_i"] + P, 0), "ki": (ZOFF["k_i"], 1), "kcmp": (ZOFF["k_cmp"], 1), "vcmp": (ZOFF["v_cmp"], 1),
       "qa0": (ZOFF["q_a"], 0), "qa1": (ZOFF["q_a"] + P, 0), "ksel": (ZOFF["k_sel"], 1), "kwin": (ZOFF["k_win"], 1),
       "qc0": (ZOFF["q_c"], 0), "qc1": (ZOFF["q_c"] + P, 0), "qd0": (ZOFF["q_d"], 0), "qd1": (ZOFF["q_d"] + P, 0),
       "kd0": (ZOFF["k_d"], 1), "kd1": (ZOFF["k_d"] + DH, 1)}
SRC_BANKS = [["qb0", "qb1"], ["kb0", "kb1"], ["qi0", "qi1"], ["ki", "kcmp"], ["vcmp"], ["qa0", "qa1"], ["ksel", "kwin"],
             ["qc0", "qc1"], ["qd0", "qd1"], ["kd0", "kd1"]]
TWINS = ["ki", "ksel", "kwin", "kd0", "kd1"]
TWINS_CMP = ["kcmp", "vcmp"]
TSLOT = {n: i for i, n in enumerate(sum(SRC_BANKS, []))}
TSLOT.update(ckv=19, kc0=20, kc1=21)
NTS = 22

UNITS = [(m, t) for m in ("fox", "sel", "win", "cmp", "swa", "dsa") for t in range(NT)]
OUT_OF = {"sel": 0, "win": 0, "cmp": 0, "fox": 1, "dsa": 2, "swa": 3}
GATE_OF = {"cmp": 0, "sel": 1, "win": 2}

WIN = [NZ - 1] + list(range(NZ - 1))
NRAW = 4
NHI = 4
PIECES = [(kind, n, half) for kind, n in
          ([("win", n) for n in WIN] + [("gate", 0), ("gate", 1), ("w1", 0), ("w1", 1)]
           + [("gate", n) for n in range(2, 8)] + [("wb", 0), ("wb", 1), ("wo", 0), ("wo", 1)]) for half in range(2)]
PIECE = {n: i for i, n in enumerate(PIECES)}
SPLIT = [p for p in PIECES if p[0] in ("win", "gate")]
SPLIT_AT = {n: i for i, n in enumerate(SPLIT)}
PLACE = [i % NRAW if i < len(PIECES) - NHI else NRAW + i - (len(PIECES) - NHI) for i in range(len(PIECES))]
ARRIVED, _cnt = [], [0] * (NRAW + NHI)
for _i, _n in enumerate(PIECES):
    if _i >= NRAW:
        _cnt[PLACE[_i]] += 16
    ARRIVED.append(_cnt[PLACE[_i]])

T_USE = (["pe"] + [("hn", t, g) for t in range(NT) for g in range(2)] + [("src", i) for i in range(5)]
         + ["ckv"] + [("src", i) for i in range(5, 10)] + ["kc", "cmph"]
         + [("p", u, i) for u, (m, t) in enumerate(UNITS) for i in range(2 if t and m != "cmp" else 1)]
         + [("o", i) for i in range(4)] + [("m", t, g) for t in range(NT) for g in range(2)]
         + [("hn2", t, g) for t in range(NT) for g in range(2)] + [("st", i) for i in range(2)]
         + [("y", s, g) for s in range(4) for g in range(2)])
T_AT = {n: i for i, n in enumerate(T_USE)}
G_USE = (["bc"] + [("z", n) for n in WIN] + ["cum", ("idx", 0), ("idx", 1), "kvc", "cmph", "cmpo"]
         + [("s", u) for u in range(len(UNITS))] + [("mg", t, n, i) for t in range(NT) for n in range(2) for i in range(2)]
         + [("wo", t) for t in range(NT)] + ["router", "tot", "pos", "blk"] + [("ga", i) for i in range(4)]
         + [("sc", t) for t in range(NT)])
G_AT = {n: i for i, n in enumerate(G_USE)}
GATES = [(n, t) for n in range(8) for t in range(NT)]

LAYER_SEMS = ("wfree", "small", "small2", "wr", "ss", "ms", "rms", "hn", "hnt", "tp", "te0", "te1", "g", "ge0", "ge1", "dve",
              "gate", "gate_out", "ahi", "alo", "nhi", "nlo", "blocks_done", "rope", "twin", "twin_cmp", "foxneg", "foxexp", "foxln", "logf", "sm", "exp", "sink", "sinkexp",
              "pv", "oc", "relu", "ckvss", "ckvms", "ckvrms", "ckvn", "kvrope", "zc", "gelu_in", "gelu_b",
              "gelu_th", "gelu", "ln_e", "logits", "gexp_in", "gexp", "texp_in", "texp", "oh", "cnt", "pos", "blk3",
              "tab", "p01", "pw", "pad", "gu", "th", "hid_a", "hid", "hid_t", "hidT", "whi", "wlo", "xh", "xl", "down", "ya", "yd", "y_all",
              "ss2", "ms2", "rms2", "hn2", "h", "gather_hi", "gather_lo")
ALL_SEMS = LAYER_SEMS + tuple(f"w{i}" for i in range(NRAW + NHI)) + tuple(
    f"e{k}{i}" for k in ("g", "u", "d") for i in range(3))


def trunk(nc, A, out):
    with ExitStack() as ctx:
        base = nc.sbuf_base
        place = {}

        def sb(name, shape, dt=F32):
            place[name] = nc.sbuf_base
            return ctx.enter_context(nc.sbuf_tensor(name, shape, dt))

        def over(name, what, shape, dt=F32R, skip=0):
            return nc.alloc_sbuf_tensor_at(name, shape, dt, offset=place[what] + skip)

        h = sb("h", [P, NT, D])
        hn = sb("hn", [P, NT, D])
        hnT = sb("hnT", [P, KC, T])
        zx = sb("zx", [P, 5288])
        ty = sb("ty", [P, NTS * T])
        gt = sb("gt", [P, NT, 4, D])
        ring = sb("ring", [P, 3 * 6144])
        ptb = sb("ptb", [P, 1024])
        kvs = sb("kvs", [P, NT, 2 * W])
        oall = sb("oall", [P, NT, 4, W])
        sel = sb("sel", [P, NT, T])
        cst = sb("cst", [P, N_CONST])
        cos = sb("cos", [P, NT, DH])
        sin = sb("sin", [P, NT, DH])
        otmp = sb("otmp", [P, W])
        wr = sb("wr", [P, KC, GROUPS + E])
        row = sb("row", [1, 80])
        bc = sb("bc", [P, 80])
        gain1 = sb("gain1", [P, KC])
        gain2 = sb("gain2", [P, KC])
        ckvg = sb("ckvg", [P, 1])
        pe_in = sb("pe_in", [CMP_LEN // 2, 2, P])
        peT = sb("peT", [P, CMP_LEN])
        small = sb("small", [P, 512])
        nmx = sb("nmx", [P, 14, H])
        ssum = sb("ssum", [P, 14, H])
        tab = sb("tab", [1, 2, NBLK], I32)
        tabf = sb("tabf", [1, 2, NBLK])

        w_hi = [over(f"w_hi{i}", "gt", [P, 2, KC, DE], skip=16384 * i) for i in range(2)]
        w_lo = [over(f"w_lo{i}", "ring", [P, 2, KC, DE], skip=24576 * i) for i in range(3)]
        a_lo = [over(f"a_lo{i}", "ring", [P, 2048], skip=8192 * i) for i in range(NRAW)]
        a_hi = [over(f"a_hi{i}", "ring", [P, 2048], skip=8192 * (NRAW + i)) for i in range(NHI)]
        hn_hi = over("hn_hi", "ring", [P, KC, T], skip=8192 * (NRAW + NHI))
        hn_lo = over("hn_lo", "hnT", [P, KC, T])
        gather_hi = over("gather_hi", "gt", [P, NT, D], skip=16384)
        gather_lo = over("gather_lo", "gt", [P, NT, D], skip=24576)
        onehot = over("onehot", "oall", [P, NT, PAIRS])
        x_hi = [over(f"x_hi{i}", w, [P, KC, BLK]) for i, w in enumerate(("hnT", "oall"))]
        x_lo = [over(f"x_lo{i}", w, [P, KC, BLK], skip=4096) for i, w in enumerate(("hnT", "oall"))]

        psT = ctx.enter_context(nc.psum_tensor("psT", [P, 2, 512], F32))
        psG = ctx.enter_context(nc.psum_tensor("psG", [P, 2, 2, 512], F32))
        psO = ctx.enter_context(nc.psum_tensor("psO", [P, 2, W], F32))
        psA = ctx.enter_context(nc.psum_tensor("psA", [P, 512], F32))

        S = {n: ctx.enter_context(nc.semaphore("s_" + n)) for n in ALL_SEMS}
        s_next = [ctx.enter_context(nc.semaphore(f"s_next{i}")) for i in range(NRAW)]
        s_next_small = ctx.enter_context(nc.semaphore("s_next_small"))
        s_pre = {n: ctx.enter_context(nc.semaphore("p_" + n)) for n in ("dma", "pos", "dve", "ang", "sin", "out",
                                                                       "ss", "ms", "rms", "g", "fin", "y")}

        def C(name):
            o, w = CONST[name]
            return cst[:, o:o + w]

        ident, ones = C("ident"), C("ones")
        causal = [C("causal")[:, P:T], C("causal")]
        swa_mask = [C("causal")[:, P:T], C("swa")]
        cmp_mask = [C("cmp")[:, N_CMP * t:N_CMP * (t + 1)] for t in range(NT)]
        z = zx[:, 0:NT * D_IN].rearrange("p (t n) -> p t n", t=NT)
        xs = zx[:, 0:KC * SLOTS].rearrange("p (k s) -> p k s", k=KC)
        tr = ty[:, :].rearrange("p (n t) -> p n t", t=T)
        oT = ty[:, 0:4 * 2 * T].rearrange("p (i c t) -> p i c t", i=4, c=2)
        yT = ty[:, 0:KC * SLOTS].rearrange("p (k s) -> p k s", k=KC)
        yn = gt[:, :, :, :].rearrange("p a b n -> p (a b n)")[:, 0:4 * D].rearrange("p (s n) -> p s n", s=4)
        ukv = gt[:, 1, 3, 512:1024]
        w2k = gt[:, 0, 3, 512:768].rearrange("p (c a d) -> p c a d", c=2, a=2)
        w2v = gt[:, 0, 3, 768:896].rearrange("p (c d) -> p c d", c=2)
        twin = gt[:, 1, 2:4].rearrange("p i n -> p (i n)")[:, 0:NT * len(TWINS) * 2 * DH].rearrange(
            "p (t n d) -> p t n d", t=NT, n=len(TWINS))
        twin_cmp = gt[:, 0, 2, 0:NT * 4 * DH].rearrange("p (t n d) -> p t n d", t=NT, n=2)
        zc = oall[:, 1].rearrange("p i w -> p (i w)")[:, 0:CMP_LEN * N_CMP].rearrange(
            "p (j c w) -> p j c w", j=2, c=CMP_LEN // 2)
        fin = ring[0:1, 0:D]
        piece = [ring[:, 2048 * i:2048 * (i + 1)] for i in range(NRAW + NHI)]
        eslot = [ring[:, 6144 * i:6144 * (i + 1)] for i in range(3)]
        sm = [hn[:, i, :].rearrange("p (h s) -> p h s", h=H) for i in range(2)]
        merged = hn
        pt = ptb[:, :].rearrange("p (h k q) -> p h k q", h=H, k=NT)
        mtmp = ptb[:, 0:512]
        stt_ = kvs[:, :, :].rearrange("p a b -> p (a b)").rearrange("p (s t) -> p s t", s=4)
        weighted = oall[:, 1].rearrange("p i w -> p (i w)").rearrange("p (t s) -> p t s", t=NT)
        th, hida = (hn[:, 0, 512 * i:512 * i + 512].rearrange("p (b n) -> p b n", b=2) for i in range(2))
        hid = hn[:, 1, 0:512].rearrange("p (b n) -> p b n", b=2)
        hidT = hn[:, 1, 512:1024].rearrange("p (b j s) -> p b j s", b=2, j=2)
        psH = [psO[:, :, :].rearrange("p a b -> p (a b)")[:, 0:2 * BLK], psA[:, 0:2 * BLK]]

        _s = [0]

        def sm_(n):
            _s[0] += n
            return small[:, _s[0] - n:_s[0]]

        ss, rms, rstd = sm_(2), sm_(2), sm_(2)
        css, crms, crstd = sm_(2), sm_(2), sm_(2)
        fx = sm_(8).rearrange("p (t h) -> p t h", t=2)
        fa = sm_(8).rearrange("p (t h) -> p t h", t=2)
        logf = sm_(8).rearrange("p (t h) -> p t h", t=2)
        wi = sm_(8).rearrange("p (t h) -> p t h", t=2)
        ga = sm_(24).rearrange("p (t h g) -> p t h g", t=2, h=H)
        m8 = sm_(8)
        coef, sinkv = sm_(H), sm_(H)
        spare = sm_(1)
        gmx, pg, v1, v2, ee, w1s, w2s, d1, d2 = (sm_(2) for _ in range(9))
        g8 = sm_(16).rearrange("p (t g) -> p t g", t=2)
        g8b = sm_(16).rearrange("p (t g) -> p t g", t=2)
        ohg = sm_(16).rearrange("p (t g) -> p t g", t=2)
        cnt, pos = sm_(2), sm_(2)
        bend, c0 = sm_(1), sm_(1)
        kcT = sm_(N_CMP)
        hcT = sm_(4 * N_CMP).rearrange("p (j c) -> p j c", j=4)
        cumT, ncumT = kvs[0:H, 0, 0:T], kvs[0:H, 0, T:2 * T]
        vc = kvs[0:N_CMP, 1, 0:DH]
        gx, gb = oall[0:N_CMP, 0, 0:2].rearrange("p i w -> p (i w)"), oall[0:N_CMP, 0, 2:4].rearrange("p i w -> p (i w)")
        vcs = sb("vcs", [N_CMP, DH])
        cumb = sb("cumb", [H, 2, T])
        lg = ptb[:, 0:144].rearrange("p (t n) -> p t n", t=2)
        em = ptb[:, 144:272].rearrange("p (t n) -> p t n", t=2)
        eq = ptb[:, 272:400].rearrange("p (t n) -> p t n", t=2)
        oh1 = ptb[:, 400:528].rearrange("p (t n) -> p t n", t=2)
        oh2 = ptb[:, 528:656].rearrange("p (t n) -> p t n", t=2)
        oh = ptb[:, 656:784].rearrange("p (t n) -> p t n", t=2)
        totbc = ptb[0:E, 784:912]
        blk3 = sel[0:E, :, :].rearrange("p a b -> p (a b)")[:, 0:3 * NBLK].rearrange("p (a b) -> p a b", a=3)

        AT = [0, 2, 1, 3]

        def by_head(a):
            return a.rearrange("p (a b) -> p b a", a=2)

        def pt_of(kt, x, s):
            j = x if kt == 1 else 2 * x + s
            return ptb[:, P * j:P * (j + 1)]

        def T_use(pe, name):
            i = T_AT[name]
            if i >= 2:
                pe.wait_ge(S[f"te{i % 2}"], i // 2)
            return psT[:, i % 2, :]

        def T_ready(eng, name):
            i = T_AT[name]
            eng.wait_ge(S["tp"], i + 1)
            return psT[:, i % 2, :], S[f"te{i % 2}"]

        def G_use(pe, name):
            i = G_AT[name]
            if i >= 2:
                pe.wait_ge(S[f"ge{i % 2}"], i // 2)
            return psG[:, i % 2]

        def G_ready(eng, name):
            i = G_AT[name]
            eng.wait_ge(S["g"], i + 1)
            return psG[:, i % 2], S[f"ge{i % 2}"]

        def T_out_upto(eng, name):
            for b in range(2):
                eng.wait_ge(S[f"te{b}"], (T_AT[name] - b) // 2 + 1)

        def G_out_upto(eng, name):
            for b in range(2):
                eng.wait_ge(S[f"ge{b}"], (G_AT[name] - b) // 2 + 1)

        def if_used(eng, i, d):
            if not isinstance(i, int) or 6 * i + d < E:
                return nullcontext()
            return eng.If(extra[6 * i + d] < PAIRS)

        def load_extra(eng):
            for b in range(E, NBLK):
                extra[b] = eng.value_load(tab[0:1, 1, b:b + 1], min_val=0, max_val=PAIRS)

        extra = {}

        def arrived(i, d):
            return 32 * i + 16 * (d // 3 + 1)

        def landed(eng, i, l):
            if i < NRAW:
                eng.wait_ge(s_next[i], 16 * l + 16)
            else:
                eng.wait_ge(S[f"w{PLACE[i]}"], ARRIVED[i])

        def width(name):
            return min(512, D_IN - 512 * name[1]) if name[0] == "win" else 512

        def a_view(a, name):
            return a[:, 0:4 * width(name)].rearrange("p (k n) -> p k n", k=4)

        def load_piece(sp, i, l, sem):
            kind, n, half = PIECES[i]
            dst = piece[PLACE[i]]

            def at(name):
                return A[name][bass.ds(l, 1)]

            if kind == "win":
                c = width(PIECES[i])
                src = at("w_in")[:, :, 512 * n:512 * n + c].rearrange("l (p k) n -> (l p) k n", k=KC)
                sp.dma_start(a_view(dst, PIECES[i]), src[:, 4 * half:4 * half + 4, :]).then_inc(sem, 16)
            elif kind == "gate":
                b, c = n // 2, 512 * (n % 2)
                src = at("w_gate")[:, b, :, c:c + 512].rearrange("l (p k) n -> (l p) k n", k=KC)
                sp.dma_start(a_view(dst, PIECES[i]), src[:, 4 * half:4 * half + 4, :]).then_inc(sem, 16)
            elif kind == "w1":
                src = at(("nsa_w1_k", "nsa_w1_v")[n]).rearrange("l (c p) n -> (l p) c n", p=P)
                sp.dma_start(dst.rearrange("p (c n) -> p c n", c=8), src[:, 8 * half:8 * half + 8, :]).then_inc(sem, 16)
            elif kind == "wb":
                sp.dma_start(dst.rearrange("p (c n) -> p c n", c=2),
                             at("w_branch")[:, 2 * n + half].rearrange("l (c p) n -> (l p) c n", p=P)).then_inc(sem, 16)
            else:
                src = at("w_out")[:, :, 512 * n:512 * n + 512].rearrange("l (p k) n -> (l p) k n", k=KC)
                sp.dma_start(a_view(dst, PIECES[i]), src[:, 4 * half:4 * half + 4, :]).then_inc(sem, 16)

        def load_ahead(sp, l):
            def small_load(dst, name, pattern=None):
                src = A[name][bass.ds(l, 1)]
                sp.dma_start(dst, src.rearrange(pattern, k=KC) if pattern == "l (p k) -> (l p) k"
                             else src.rearrange(pattern, a=2) if pattern else src).then_inc(s_next_small, 16)

            small_load(gain1[:, :], "attn_norm", "l (p k) -> (l p) k")
            small_load(row[0:1, 0:8], "moe_b_group")
            small_load(row[0:1, 8:72], "moe_b_expert")
            small_load(row[0:1, 72:76], "fox_forget_bias")
            small_load(row[0:1, 76:80], "swa_sinks")
            for j, name in enumerate(("nsa_pe_k", "nsa_pe_v")):
                small_load(pe_in[:, j, :], name, "l (c a) d -> (l c) (a d)")
            for i in range(NRAW):
                load_piece(sp, i, l, s_next[i])

        posi = small[:, 500:502].bitcast(I32)
        posf = small[:, 502:504]
        ang = ptb[:, 0:64].rearrange("p (t f) -> p t f", t=NT)
        kk = ptb[:, 64:128].rearrange("p (t f) -> p t f", t=NT)
        sn = ptb[:, 128:192].rearrange("p (t f) -> p t f", t=NT)
        sh = ptb[:, 192:256].rearrange("p (t f) -> p t f", t=NT)

        with nc.Block() as block:
            @block.sync
            def _(sp):
                sp.dma_start(cst[:, :], A["consts"]).then_inc(s_pre["dma"], 16)
                for t in range(NT):
                    sp.dma_start(posi[:, t:t + 1], A["positions"][0:1, t * P:(t + 1) * P].rearrange("a p -> p a")
                                 ).then_inc(s_pre["dma"], 16)
                sp.dma_start(h[:, :, :], A["x"][0].rearrange("(t p) d -> p t d", p=P)).then_inc(s_pre["dma"], 16)
                load_ahead(sp, 0)
                sp.wait_ge(s_pre["dma"], 64)

            @block.vector
            def _(dve):
                n = [0]

                def link(ins):
                    n[0] += 1
                    ins.then_inc(s_pre["dve"], 1)
                    dve.wait_ge(s_pre["dve"], n[0])

                dve.wait_ge(s_pre["dma"], 64)
                link(dve.tensor_copy(posf, posi))
                for t in range(NT):
                    link(dve.tensor_scalar(ang[:, t], C("inv_freq"), posf[:, t:t + 1], None, ALU.mult))
                magic, two_pi = 12582912.0, 2 * np.pi
                c1 = 6.28125
                c2 = float(np.float32(np.round((two_pi - c1) * 2 ** 20) / 2 ** 20))
                c3 = float(np.float32(two_pi - c1 - c2))
                link(dve.tensor_scalar(kk, ang, 1 / two_pi, magic, ALU.mult, ALU.add))
                link(dve.tensor_scalar(kk, kk, -magic, None, ALU.add))
                for c in (c1, c2, c3):
                    link(dve.scalar_tensor_tensor(out=ang, in0=kk, scalar=-c, in1=ang, op0=ALU.mult, op1=ALU.add))
                dve.tensor_scalar(ang, ang, 3.1415925, -3.1415925, ALU.min, ALU.max).then_inc(s_pre["ang"], 1)
                dve.wait_ge(s_pre["sin"], 2)
                link(dve.tensor_tensor(kk, sh, sh, ALU.mult))
                for half in range(2):
                    link(dve.tensor_scalar(cos[:, :, 32 * half:32 * half + 32], kk, -2.0, 1.0, ALU.mult, ALU.add))
                link(dve.tensor_scalar(sin[:, :, 0:32], sn, -1.0, None, ALU.mult))
                link(dve.tensor_copy(sin[:, :, 32:64], sn))

            @block.scalar
            def _(act):
                act.wait_ge(s_pre["ang"], 1)
                act.activation(sn, ang, ACT.Sin).then_inc(s_pre["sin"], 1)
                act.activation(sh, ang, ACT.Sin, scale=0.5).then_inc(s_pre["sin"], 1)

        with nc.Fori(0, DEPTH) as l:
            def at(name):
                a = A[name]
                return a[bass.ds(l, 1)]

            with nc.Block() as block:
                @block.sync
                def _(sp):
                    def small_load(dst, src, s):
                        sp.dma_start(dst, src).then_inc(S[s], 16)

                    sp.wait_ge(s_next_small, 112 * l + 112)
                    sp.sem_inc(S["small"], 1)
                    small_load(gain2[:, :], at("ffn_norm").rearrange("l (p k) -> (l p) k", k=KC), "small2")
                    small_load(ckvg[:, :], at("dsa_kv_norm").rearrange("l (p a) -> (l p) a", a=1), "small2")
                    small_load(ukv[:, :], at("dsa_w_ukv").rearrange("l p n -> (l p) n"), "small2")
                    for j in range(2):
                        small_load(w2k[:, :, j, :], at("nsa_w2_k").rearrange("l (c p) d -> (l p) c d", p=P), "small2")
                    small_load(w2v[:, :, :], at("nsa_w2_v").rearrange("l (c p) d -> (l p) c d", p=P), "small2")
                    small_load(wr[:, :, 0:GROUPS], at("moe_w_group").rearrange("l (p k) n -> (l p) k n", k=KC), "small2")
                    small_load(wr[:, :, GROUPS:], at("moe_w_expert").rearrange("l (p k) n -> (l p) k n", k=KC), "small2")
                    for i in range(NRAW, len(PIECES)):
                        last = max([j for j in range(i) if PLACE[j] == PLACE[i]], default=PIECE[("gate", 7, 1)])
                        sp.wait_ge(S["wfree"], last + 1)
                        load_piece(sp, i, l, S[f"w{PLACE[i]}"])

                    def load_block(b, j, wait=None):
                        e = sp.value_load(tab[0:1, 0, bass.ds(b, 1)], min_val=0, max_val=E - 1)
                        for k, (name, r) in enumerate((("moe_w_gate", KC), ("moe_w_up", KC), ("moe_w_down", 2))):
                            if wait is not None and k == 0:
                                sp.wait_ge(S["gu"], wait)
                            if wait is not None and k == 2:
                                sp.wait_ge(S["down"], wait)
                            src = A[name][bass.ds(l, 1), bass.ds(e, 1)].rearrange("l e (p k) n -> (l e p) (k n)", k=r)
                            sp.dma_start(eslot[j][:, 2048 * k:2048 * (k + 1)], src).then_inc(S[f"e{'gud'[k]}{j}"], 16)

                    sp.wait_ge(S["tab"], 1)
                    sp.wait_ge(S["wfree"], len(PIECES))
                    for j in range(3):
                        load_block(j, j)
                    with sp.Fori(1, E // 3) as i:
                        for j in range(3):
                            load_block(3 * i + j, j, 3 * i + (j - 2))
                    load_extra(sp)
                    for b in range(3 * (E // 3), NBLK):
                        with if_used(sp, 0, b):
                            load_block(b, b % 3, b - 2)
                    with sp.If(l < DEPTH - 1):
                        sp.wait_ge(S["blocks_done"], 1)
                        load_ahead(sp, nc.s_assert_within(l + 1, 1, DEPTH - 1,
                                                          skip_runtime_bounds_check_because="the If holds l below DEPTH - 1"))

                @block.tensor
                def _(pe):
                    def transposes(name, ins):
                        bank = T_use(pe, name)
                        w = 0
                        for a in ins:
                            n = a.shape[0]
                            m = pe.transpose(bank[0:a.shape[-1], w:w + n], a, ident[0:n, 0:n])
                            w += P if n == P else N_CMP if n == N_CMP else n
                        m.then_inc(S["tp"], 1)

                    gate_at = [0]

                    def gate_units(n):
                        for _ in range(n):
                            if gate_at[0] == len(GATES):
                                return
                            i, t = GATES[gate_at[0]]
                            if gate_at[0]:
                                pe.wait_ge(S["gate_out"], gate_at[0])
                            hn_times(("gate", i), t, psA[:, :]).then_inc(S["gate"], 1)
                            gate_at[0] += 1
                            if t:
                                pe.wait_ge(S["gate"], gate_at[0])
                                pe.sem_inc(S["wfree"], 1)

                    def hn_times(name, t, o):
                        for half in range(2):
                            q = SPLIT_AT[(*name, half)]
                            hi, lo = a_view(a_hi[q % NHI], name), a_view(a_lo[PLACE[PIECE[(*name, half)]]], name)
                            for part, (x, w) in enumerate(((hn_hi, hi), (hn_lo, hi), (hn_hi, lo))):
                                if not t and part == 0:
                                    pe.wait_ge(S["ahi"], q + 1)
                                if not t and part == 2:
                                    pe.wait_ge(S["alo"], q + 1)
                                for k in range(4):
                                    m = pe.matmul(o, x[:, 4 * half + k, t * P:(t + 1) * P], w[:, k, :],
                                                  start=(half == part == k == 0), stop=(half == 1 and part == 2 and k == 3))
                            if t and not half:
                                m.then_inc(S["wfree"], 1)
                        return m

                    pe.wait_ge(S["small"], 1)
                    transposes("pe", [pe_in[:, j, :] for j in range(2)])
                    g = G_use(pe, "bc")
                    pe.matmul(g[:, 0, 0:80], ones[0:1, :], row[0:1, :], start=True, stop=True).then_inc(S["g"], 1)
                    for t in range(NT):
                        pe.wait_ge(S["hn"], t + 1)
                        for q in range(2):
                            transposes(("hn", t, q), [hn[:, t, k:D:KC] for k in range(4 * q, 4 * q + 4)])
                    pe.wait_ge(S["nhi"], 4)
                    pe.wait_ge(S["nlo"], 4)
                    for n in WIN:
                        g = G_use(pe, ("z", n))
                        for t in range(NT):
                            m = hn_times(("win", n), t, g[:, t, 0:width(("win", n))])
                        m.then_inc(S["g"], 1)
                        pe.wait_ge(S["g"], G_AT[("z", n)] + 1)
                        pe.sem_inc(S["wfree"], 1)

                    def head_T(name, t=None):
                        a = tr[:, TSLOT[name], :]
                        return a if t is None else a[:, t * P:(t + 1) * P]

                    def src(name, t):
                        c, twice = SRC[name]
                        if name in TWINS_CMP:
                            return twin_cmp[:, t, TWINS_CMP.index(name), :]
                        if twice:
                            return twin[:, t, TWINS.index(name), :]
                        return z[:, t, c:c + P]

                    def src_T(i):
                        bank = T_use(pe, ("src", i))
                        w = 0
                        for name in SRC_BANKS[i]:
                            for t in range(NT):
                                m = pe.transpose(bank[:, w:w + P], src(name, t), ident)
                                w += P
                        m.then_inc(S["tp"], 1)

                    gate_units(2)
                    G_out_upto(pe, ("z", WIN[-1]))
                    src_T(0)
                    src_T(1)
                    pe.wait_ge(S["logf"], 1)
                    g = G_use(pe, "cum")
                    pe.matmul(g[0:H, 0, 0:P], logf[:, 0, :], C("upto"), start=True, stop=True)
                    pe.matmul(g[0:H, 1, 0:P], logf[:, 0, :], ones, start=True, stop=False)
                    pe.matmul(g[0:H, 1, 0:P], logf[:, 1, :], C("upto"), start=False, stop=True).then_inc(S["g"], 1)
                    gate_units(1)
                    pe.wait_ge(S["rope"], 2)
                    src_T(2)
                    pe.wait_ge(S["twin"], 1)
                    pe.wait_ge(S["twin_cmp"], 2)
                    src_T(3)
                    src_T(4)

                    def scores(g, t, q, k, w):
                        for x in range(H):
                            lo = DH * (x % 2)
                            m = pe.matmul(g[:, x % 2, T * (x // 2):T * (x // 2) + w],
                                          head_T(q[x // 2], t)[lo:lo + DH, :], k(x)[lo:lo + DH, 0:w], start=True, stop=True)
                        return m

                    T_out_upto(pe, ("src", 3))
                    for t in range(NT):
                        g = G_use(pe, ("idx", t))
                        scores(g, t, ("qi0", "qi1"), lambda x: head_T("ki"), P * (t + 1)).then_inc(S["g"], 1)
                    pe.wait_ge(S["ckvn"], 1)
                    pe.wait_ge(S["small2"], 16 * 8)
                    transposes("ckv", [kvs[:, t, 0:P] for t in range(NT)])
                    gate_units(1)
                    T_out_upto(pe, "ckv")
                    g = G_use(pe, "kvc")
                    for t in range(NT):
                        m = pe.matmul(g[:, t, :], head_T("ckv", t), ukv[:, :], start=True, stop=True)
                    m.then_inc(S["g"], 1)
                    pe.wait_ge(S["twin"], len(TWINS))
                    for i in range(5, 10):
                        src_T(i)
                    pe.wait_ge(S["kvrope"], 1)
                    bank = T_use(pe, "kc")
                    for i in range(2):
                        for t in range(NT):
                            m = pe.transpose(bank[:, P * (2 * i + t):P * (2 * i + t + 1)], kvs[:, t, P * i:P * (i + 1)],
                                             ident)
                    m.then_inc(S["tp"], 1)
                    pe.wait_ge(S["zc"], 1)
                    g = G_use(pe, "cmph")
                    for n in range(2):
                        w = [piece[PLACE[PIECE[("w1", n, half)]]].rearrange("p (c n) -> p c n", n=CMP_HID)
                             for half in range(2)]
                        for half in range(2):
                            landed(pe, PIECE[("w1", n, half)], l)
                        for c in range(16):
                            m = pe.matmul(g[0:N_CMP, n, 0:CMP_HID], zc[:, n, c, :], w[c // 8][:, c % 8, :],
                                          start=(c == 0), stop=(c == 15))
                        m.then_inc(S["wfree"], 2)
                    pe.wait_ge(S["wfree"], PIECE[("w1", 1, 1)] + 1)
                    pe.sem_inc(S["g"], 1)
                    gate_units(2)
                    pe.wait_ge(S["gelu"], 1)
                    transposes("cmph", [gx[:, P * j:P * (j + 1)] for j in range(4)])
                    T_out_upto(pe, "cmph")
                    g = G_use(pe, "cmpo")
                    for c in range(2):
                        pe.matmul(g[:, 0, 0:N_CMP], w2k[:, c].rearrange("p a d -> p (a d)"), hcT[:, c, :],
                                  start=(c == 0), stop=(c == 1))
                    for c in range(2):
                        m = pe.matmul(g[0:N_CMP, 1, 0:DH], hcT[:, 2 + c, :], w2v[:, c, :],
                                      start=(c == 0), stop=(c == 1))
                    m.then_inc(S["g"], 1)

                    def unit_scores(u):
                        m_, t = UNITS[u]
                        w = P * (t + 1)
                        g = G_use(pe, ("s", u))
                        if m_ == "fox":
                            for x in range(H):
                                lo = DH * (x % 2)
                                o = g[:, x % 2, T * (x // 2):T * (x // 2) + w]
                                pe.matmul(o, head_T(f"qb{x // 2}", t)[lo:lo + DH, :],
                                          head_T(f"kb{x // 2}")[lo:lo + DH, 0:w], start=True, stop=False)
                                e8 = C("eye8")[0:H, x:x + 1]
                                pe.matmul(o, cumb[:, 0, t * P:(t + 1) * P], e8.broadcast_to([H, w]),
                                          start=False, stop=False)
                                m = pe.matmul(o, e8.broadcast_to([H, P]), cumb[:, 1, 0:w], start=False, stop=True)
                        elif m_ == "cmp":
                            for x in range(H):
                                lo = DH * (x % 2)
                                m = pe.matmul(g[:, x % 2, T * (x // 2):T * (x // 2) + N_CMP],
                                              head_T(f"qa{x // 2}", t)[lo:lo + DH, :], kcT[lo:lo + DH, :],
                                              start=True, stop=True)
                        else:
                            q = {"sel": "qa", "win": "qa", "swa": "qd", "dsa": "qc"}[m_]
                            k = {"sel": lambda x: head_T("ksel"), "win": lambda x: head_T("kwin"),
                                 "swa": lambda x: head_T(f"kd{x // 2}"), "dsa": lambda x: head_T(f"kc{x // 2}")}[m_]
                            m = scores(g, t, (q + "0", q + "1"), k, w)
                        m.then_inc(S["g"], 1)

                    def unit_pt(u):
                        m_, t = UNITS[u]
                        pe.wait_ge(S["exp"], H * (u + 1))
                        kt = NT if t and m_ != "cmp" else 1
                        w = N_CMP if m_ == "cmp" else P
                        for i in range(kt):
                            bank = T_use(pe, ("p", u, i))
                            for j in range(4):
                                x, s = (j, 0) if kt == 1 else (2 * i + j // 2, j % 2)
                                mm = pe.transpose(bank[0:w, P * j:P * (j + 1)], sm[u % 2][:, AT[x], P * s:P * s + w], ident)
                            mm.then_inc(S["tp"], 1)
                        return kt

                    def unit_pv(u, kt):
                        m_, t = UNITS[u]
                        if u:
                            pe.wait_ge(S["oc"], u)
                        i = T_AT[("p", u, kt - 1)]
                        for j in range(kt):
                            pe.wait_ge(S[f"te{(i - j) % 2}"], (i - j) // 2 + 1)
                        for x in range(H):
                            for s in range(kt):
                                if m_ == "fox":
                                    v = z[:, s, ZOFF["v_b"] + DH * x:ZOFF["v_b"] + DH * (x + 1)]
                                elif m_ == "swa":
                                    c = ZOFF["v_d"] + DH * (x // 2)
                                    v = z[:, s, c:c + DH]
                                elif m_ == "dsa":
                                    v = kvs[:, s, W + DH * x:W + DH * (x + 1)]
                                elif m_ == "cmp":
                                    v = vcs[:, :]
                                else:
                                    c = ZOFF["v_" + m_]
                                    v = z[:, s, c:c + DH]
                                w = N_CMP if m_ == "cmp" else P
                                lhs = pt_of(kt, x, s)[0:w]
                                mm = pe.matmul(psO[:, u % 2, DH * x:DH * (x + 1)], lhs, v, start=(s == 0), stop=(s == kt - 1))
                        mm.then_inc(S["pv"], 1)

                    NU = len(UNITS)
                    T_out_upto(pe, "kc")
                    G_out_upto(pe, "cmpo")
                    unit_scores(0)
                    for u in range(NU):
                        if u + 1 < NU:
                            unit_scores(u + 1)
                        kt = unit_pt(u)
                        gate_units(1)
                        unit_pv(u, kt)
                    gate_units(16)
                    pe.wait_ge(S["oc"], NU)
                    for i in range(4):
                        transposes(("o", i), [oall[:, t, i, P * c:P * (c + 1)] for c in range(2) for t in range(NT)])
                    T_out_upto(pe, ("o", 3))
                    for t in range(NT):
                        for n in range(2):
                            for i2 in range(2):
                                g = G_use(pe, ("mg", t, n, i2))
                                for j in range(2):
                                    i = PIECE[("wb", i2, j)]
                                    landed(pe, i, l)
                                    w = piece[PLACE[i]].rearrange("p (c n) -> p c n", c=2)
                                    for c in range(2):
                                        m = pe.matmul(g[:, j, :], oT[:, 2 * i2 + j, c, t * P:(t + 1) * P],
                                                      w[:, c, 512 * n:512 * n + 512], start=(c == 0), stop=(c == 1))
                                m.then_inc(S["g"], 1)
                    for t in range(NT):
                        G_out_upto(pe, ("mg", t, 1, 1))
                        for q in range(2):
                            transposes(("m", t, q), [merged[:, t, k:D:KC] for k in range(4 * q, 4 * q + 4)])
                        T_out_upto(pe, ("m", t, 1))
                        g = G_use(pe, ("wo", t))
                        for n in range(2):
                            for k in range(KC):
                                i = PIECE[("wo", n, k // 4)]
                                landed(pe, i, l)
                                m = pe.matmul(g[:, n, :], hnT[:, k, t * P:(t + 1) * P],
                                              a_view(piece[PLACE[i]], ("wo", n))[:, k % 4, :],
                                              start=(k == 0), stop=(k == KC - 1))
                        m.then_inc(S["g"], 1)
                    pe.wait_ge(S["g"], G_AT[("wo", 1)] + 1)
                    pe.sem_inc(S["wfree"], 8)

                    for t in range(NT):
                        pe.wait_ge(S["hn2"], t + 1)
                        for q in range(2):
                            transposes(("hn2", t, q), [hn[:, t, k:D:KC] for k in range(4 * q, 4 * q + 4)])
                    pe.wait_ge(S["hnt"], 8)
                    g = G_use(pe, "router")
                    for t in range(NT):
                        for k in range(KC):
                            pe.matmul(g[:, t, 0:GROUPS + E], hnT[:, k, t * P:(t + 1) * P], wr[:, k, :],
                                      start=(k == 0), stop=False)
                        m = pe.matmul(g[:, t, 0:GROUPS + E], ones[0:1, :], row[0:1, 0:GROUPS + E], start=False, stop=True)
                    m.then_inc(S["g"], 1)
                    pe.wait_ge(S["oh"], 1)
                    g = G_use(pe, "tot")
                    for t in range(NT):
                        m = pe.matmul(g[0:E, 0, 0:1], oh[:, t, :], ones[:, 0:1], start=(t == 0), stop=(t == NT - 1))
                    m.then_inc(S["g"], 1)
                    pe.wait_ge(S["cnt"], 1)
                    g = G_use(pe, "pos")
                    before = C("before")
                    pe.matmul(g[0:E, 0, 0:2], before[0:E, 0:E], cnt[0:E, :], start=True, stop=True)
                    for t in range(NT):
                        o = g[:, 1, E * t:E * (t + 1)]
                        pe.matmul(o, totbc, before[0:E, 0:E], start=True, stop=False)
                        if t:
                            pe.matmul(o, ones, oh[:, 0, :], start=False, stop=False)
                        m = pe.matmul(o, before, oh[:, t, :], start=False, stop=True)
                    m.then_inc(S["g"], 1)
                    pe.wait_ge(S["blk3"], 1)
                    g = G_use(pe, "blk")
                    pe.matmul(g[0:1, 0, 0:3 * NBLK], ones[0:E, 0:1], blk3.rearrange("p a b -> p (a b)"),
                              start=True, stop=True).then_inc(S["g"], 1)
                    pe.wait_ge(S["p01"], 1)
                    pe.wait_ge(S["gather_lo"], NT)
                    for i in range(4):
                        g = G_use(pe, ("ga", i))
                        for j in range(2):
                            for t in range(NT):
                                for part in (gather_hi, gather_lo):
                                    m = pe.matmul(g[:, j, :], part[:, t, 2 * i + j:D:KC], onehot[:, t, :],
                                                  start=(t == 0 and part is gather_hi),
                                                  stop=(t == NT - 1 and part is gather_lo))
                        m.then_inc(S["g"], 1)
                    pe.wait_ge(S["pw"], 1)
                    for i in range(2):
                        transposes(("st", i), [weighted[:, t, P * s:P * (s + 1)] for s in (2 * i, 2 * i + 1)
                                               for t in range(NT)])

                    def products(j3, j2, parts):
                        for x, w in parts:
                            for c in range(KC):
                                m = pe.matmul(psT[:, j2, :], (x_hi, x_lo)[x][j2][:, c, :],
                                              (w_hi[j2], w_lo[j3])[w][:, :, c, :],
                                              start=(x == w == c == 0), stop=(w == 1 and c == KC - 1))
                        return m

                    def gate_up_hi(n, j3, j2):
                        pe.wait_ge(S["whi"], 2 * n)
                        pe.wait_ge(S["xh"], n)
                        products(j3, j2, [(0, 0)])
                        pe.wait_ge(S["xl"], n)
                        products(j3, j2, [(1, 0)])

                    def gate_up_lo(n, j3, j2):
                        pe.wait_ge(S["wlo"], 2 * n)
                        products(j3, j2, [(0, 1)]).then_inc(S["gu"], 1)

                    def turn_hidden(n, j2):
                        pe.wait_ge(S["hid"], n)
                        for j in range(2):
                            m = pe.transpose(psH[j2][:, BLK * j:BLK * (j + 1)], hid[:, j2, j:DE:2], ident)
                        m.then_inc(S["hid_t"], 1)

                    def down(n, j3, j2, arrived):
                        w = eslot[j3][:, 4096:6144].rearrange("p (j n) -> p j n", j=2)
                        pe.wait_ge(S[f"ed{j3}"], arrived)
                        pe.wait_ge(S["hidT"], n)
                        pe.wait_ge(S["ya"], n)
                        pe.wait_ge(S["yd"], n)
                        for k in range(8):
                            for j in range(2):
                                m = pe.matmul(psG[:, j2, k // 4, BLK * (k % 4):BLK * (k % 4 + 1)],
                                              w[:, j, P * k:P * (k + 1)], hidT[:, j2, j, :], start=(j == 0), stop=(j == 1))
                        m.then_inc(S["down"], 1)

                    G_out_upto(pe, ("ga", 3))
                    T_out_upto(pe, ("st", 1))
                    pe.wait_ge(S["pad"], 1)
                    pe.wait_ge(S["tab"], 1)
                    pe.sem_inc(S["ya"], 2)
                    pe.sem_inc(S["yd"], 2)

                    def pe_block(i, d, last=False):
                        if not last:
                            with if_used(pe, i, d + 1):
                                gate_up_hi(6 * i + (d + 2), (d + 1) % 3, (d + 1) % 2)
                        with if_used(pe, i, d):
                            turn_hidden(6 * i + (d + 1), d % 2)
                        if not last:
                            with if_used(pe, i, d + 1):
                                gate_up_lo(6 * i + (d + 2), (d + 1) % 3, (d + 1) % 2)
                        with if_used(pe, i, d):
                            down(6 * i + (d + 1), d % 3, d % 2, arrived(i, d))

                    gate_up_hi(1, 0, 0)
                    gate_up_lo(1, 0, 0)
                    load_extra(pe)
                    with pe.Fori(0, N_LOOP) as i:
                        for d in range(6):
                            pe_block(i, d)
                    for d in range(N_TAIL):
                        pe_block(N_LOOP, d, d == N_TAIL - 1)
                    pe.drain().then_inc(S["blocks_done"], 1)
                    pe.wait_ge(S["y_all"], 2)
                    for s in range(4):
                        for q in range(2):
                            transposes(("y", s, q), [yT[:, n, P * s:P * (s + 1)] for n in range(4 * q, 4 * q + 4)])
                    T_out_upto(pe, ("y", 3, 1))
                    for t in range(NT):
                        g = G_use(pe, ("sc", t))
                        for n in range(2):
                            for s in range(4):
                                m = pe.matmul(g[:, n, :], stt_[:, s, t * P:(t + 1) * P], yn[:, s, 512 * n:512 * n + 512],
                                              start=(s == 0), stop=(s == 3))
                        m.then_inc(S["g"], 1)

                @block.scalar
                def _(act):
                    def T_out(name, dst, n=512, p=P, scale=1.0):
                        bank, done = T_ready(act, name)
                        act.activation(dst, bank[0:p, 0:n], ACT.Copy, scale=scale).then_inc(done, 1)

                    gate_at = [0]

                    def gate_units(n):
                        for _ in range(n):
                            if gate_at[0] == len(GATES):
                                return
                            i, t = GATES[gate_at[0]]
                            act.wait_ge(S["gate"], gate_at[0] + 1)
                            act.activation(gt[:, t, i // 2, 512 * (i % 2):512 * (i % 2) + 512], psA[:, :], ACT.Tanh,
                                           scale=0.5).then_inc(S["gate_out"], 1)
                            if not t and i != 1:
                                due.append(NZ + i + 1)
                            gate_at[0] += 1

                    def round_piece(q):
                        if q >= len(SPLIT):
                            return
                        i = PIECE[SPLIT[q]]
                        landed(act, i, l)
                        if q >= NHI:
                            act.wait_ge(S["wfree"], PIECE[SPLIT[q - NHI]] + 1)
                        c = 4 * width(SPLIT[q])
                        act.activation(a_hi[q % NHI][:, 0:c], piece[PLACE[i]][:, 0:c], ACT.Copy).then_inc(S["ahi"], 1)

                    def src_out(i):
                        n, a = len(SRC_BANKS[i]), TSLOT[SRC_BANKS[i][0]]
                        T_out(("src", i), tr[:, a:a + n, :].rearrange("p n t -> p (n t)"), n * T)

                    due = []

                    def round_due():
                        while due:
                            round_item(due.pop())

                    def round_item(i):
                        for half in range(2):
                            round_piece(2 * i + half)

                    act.activation(spare, ones[:, 0:1], ACT.Sqrt)
                    T_out("pe", peT[:, :], CMP_LEN)
                    for t in range(NT):
                        act.activation(hn[:, t, :], h[:, t, :], ACT.Square, accum_out=ss[:, t:t + 1]).then_inc(S["ss"], 1)
                    act.wait_ge(S["ms"], 1)
                    act.activation(rms, rms, ACT.Sqrt).then_inc(S["rms"], 1)
                    round_piece(0)
                    for t in range(NT):
                        for q in range(2):
                            act.wait_ge(S["hnt"], 2 * t + q + 1)
                            act.activation(hn_hi[:, 4 * q:4 * q + 4, t * P:(t + 1) * P],
                                           hnT[:, 4 * q:4 * q + 4, t * P:(t + 1) * P], ACT.Copy).then_inc(S["nhi"], 1)
                    round_piece(1)
                    for i, n in enumerate(WIN):
                        round_item(i + 1)
                        c = min(512, D_IN - 512 * n)
                        g, done = G_ready(act, ("z", n))
                        act.activation(z[:, :, 512 * n:512 * n + c], g[:, :, 0:c], ACT.Copy).then_inc(done, 1)
                    for t in range(NT):
                        if not t:
                            G_out_upto(act, ("z", WIN[-1]))
                        act.activation(kvs[:, t, 0:P], z[:, t, ZOFF["ckv"]:ZOFF["ckv"] + P], ACT.Square,
                                       accum_out=css[:, t:t + 1]).then_inc(S["ckvss"], 1)
                    act.wait_ge(S["ckvms"], 1)
                    act.activation(crms, crms, ACT.Sqrt).then_inc(S["ckvrms"], 1)
                    act.wait_ge(S["foxneg"], 1)
                    act.activation(fa, fa, ACT.Exp).then_inc(S["foxexp"], 1)
                    act.wait_ge(S["foxexp"], 1)
                    act.activation(fa, fa, ACT.Ln, bias=1.0).then_inc(S["foxln"], 1)
                    act.activation(ga, z[:, :, ZOFF["g_a"]:ZOFF["g_a"] + 12].rearrange("p t (h g) -> p t h g", h=H),
                                   ACT.Tanh, scale=0.5).then_inc(S["foxln"], 1)
                    gate_units(2)
                    round_due()
                    for i in range(2):
                        src_out(i)
                    g, done = G_ready(act, "cum")
                    act.activation(cumb[:, 0, :].rearrange("p (a b) -> p a b", a=2), g[0:H, :, 0:P], ACT.Copy)
                    act.activation(cumb[:, 1, :].rearrange("p (a b) -> p a b", a=2), g[0:H, :, 0:P], ACT.Copy,
                                   scale=-1.0).then_inc(done, 1)
                    gate_units(1)
                    for i in range(2, 5):
                        src_out(i)
                    for t in range(NT):
                        w = P * (t + 1)
                        g, done = G_ready(act, ("idx", t))
                        act.activation(sm[t][:, :, 0:w], g.rearrange("p a (b s) -> p (a b) s", b=2)[:, :, 0:w],
                                       ACT.Relu, scale=SCALE).then_inc(done, 1)
                    act.wait_ge(S["small2"], 16 * 8)
                    bank, done = T_ready(act, "ckv")
                    act.activation(tr[:, TSLOT["ckv"], :], bank[:, 0:T], ACT.Copy, scale=ckvg[:, 0:1]).then_inc(done, 1)
                    gate_units(1)
                    g, done = G_ready(act, "kvc")
                    act.activation(kvs[:, :, :], g, ACT.Copy).then_inc(done, 1)
                    for i in range(5, 10):
                        src_out(i)
                    T_out("kc", tr[:, 20:22, :].rearrange("p n t -> p (n t)"))
                    round_item(NZ + 2)
                    g, done = G_ready(act, "cmph")
                    act.activation(gx.rearrange("p (a b) -> p a b", a=2), g[0:N_CMP, :, 0:CMP_HID], ACT.Copy)
                    act.activation(gb.rearrange("p (a b) -> p a b", a=2), g[0:N_CMP, :, 0:CMP_HID], ACT.Square)\
                        .then_inc(done, 1)
                    act.wait_ge(S["gelu_b"], 1)
                    act.activation(gb, gb, ACT.Tanh, scale=GELU_C).then_inc(S["gelu_th"], 1)
                    gate_units(2)
                    bank, done = T_ready(act, "cmph")
                    act.activation(hcT.rearrange("p j c -> p (j c)"), bank[:, 0:4 * N_CMP], ACT.Copy, scale=0.5)\
                        .then_inc(done, 1)
                    g, done = G_ready(act, "cmpo")
                    act.activation(kcT, g[:, 0, 0:N_CMP], ACT.Copy)
                    act.activation(vcs[:, :], g[0:N_CMP, 1, 0:DH], ACT.Copy).then_inc(done, 1)
                    round_due()

                    NU = len(UNITS)

                    def exps(u):
                        m_, t = UNITS[u]
                        w = N_CMP if m_ == "cmp" else P * (t + 1)
                        act.wait_ge(S["sm"], u + 1)
                        for x in range(H):
                            act.activation(sm[u % 2][:, x, 0:w], sm[u % 2][:, x, 0:w], ACT.Exp, bias=nmx[:, u, x:x + 1],
                                           accum_out=ssum[:, u, x:x + 1]).then_inc(S["exp"], 1)
                        if m_ == "swa":
                            act.wait_ge(S["sink"], t + 1)
                            act.activation(ssum[:, 12 + t, :], nmx[:, 12 + t, :], ACT.Exp).then_inc(S["sinkexp"], 1)

                    exps(0)
                    for u, (m_, t) in enumerate(UNITS):
                        kt = NT if t and m_ != "cmp" else 1
                        wp = N_CMP if m_ == "cmp" else P
                        if u:
                            act.wait_ge(S["pv"], u)
                        for i in range(kt):
                            T_out(("p", u, i), ptb[0:wp, 512 * i:512 * (i + 1)], 512, wp)
                        if u + 1 < NU:
                            exps(u + 1)
                        gate_units(1)
                        round_due()
                    gate_units(16)
                    for i in range(4):
                        T_out(("o", i), oT[:, i].rearrange("p c t -> p (c t)"))
                    for t in range(NT):
                        for q in range(2):
                            T_out(("m", t, q), hnT[:, 4 * q:4 * q + 4, t * P:(t + 1) * P], scale=0.5)
                    act.activation(spare, ones[:, 0:1], ACT.Sqrt)
                    for t in range(NT):
                        act.wait_ge(S["h"], t + 1)
                        act.activation(hn[:, t, :], h[:, t, :], ACT.Square, accum_out=ss[:, t:t + 1]).then_inc(S["ss2"], 1)
                        act.wait_ge(S["ms2"], t + 1)
                        act.activation(rms[:, t:t + 1], rms[:, t:t + 1], ACT.Sqrt).then_inc(S["rms2"], 1)
                        act.wait_ge(S["hn2"], t + 1)
                        act.activation(gather_hi[:, t, :], hn[:, t, :], ACT.Copy).then_inc(S["gather_hi"], 1)
                    act.wait_ge(S["gexp_in"], 1)
                    act.activation(g8b, g8b, ACT.Exp).then_inc(S["gexp"], 1)
                    act.wait_ge(S["texp_in"], 1)
                    act.activation(ee, ee, ACT.Exp).then_inc(S["texp"], 1)
                    def round_input(b, j2):
                        c = act.value_load(tab[0:1, 1, bass.ds(b, 1)], min_val=0, max_val=PAIRS)
                        act.activation(x_hi[j2][:, :, :], xs[:, :, bass.ds(c, BLK)], ACT.Copy).then_inc(S["xh"], 1)

                    def round_weights(k, j3, j2, arrived):
                        act.wait_ge(S[f"e{'gu'[k]}{j3}"], arrived)
                        act.activation(w_hi[j2][:, k], eslot[j3][:, 2048 * k:2048 * (k + 1)].rearrange(
                            "p (k n) -> p k n", k=KC), ACT.Copy).then_inc(S["whi"], 1)

                    for i in (0, 2):
                        g, done = G_ready(act, ("ga", i))
                        act.activation(xs[:, 2 * i, 0:PAIRS], g[:, 0, :], ACT.Copy, scale=gain2[:, 2 * i:2 * i + 1])
                        act.activation(xs[:, 2 * i + 1, 0:PAIRS], g[:, 1, :], ACT.Copy,
                                       scale=gain2[:, 2 * i + 1:2 * i + 2]).then_inc(done, 1)
                    for k in range(2):
                        round_weights(k, 0, 0, 16)
                    act.wait_ge(S["pad"], 1)
                    G_out_upto(act, ("ga", 3))
                    round_input(0, 0)


                    def tanh_gate(n, j2):
                        act.wait_ge(S["gu"], n)
                        act.activation(th[:, j2], psT[:, j2, 0:DE], ACT.Tanh, scale=0.5).then_inc(S["th"], 1)

                    def hidden_out(n, j2):
                        act.wait_ge(S["hid_t"], n)
                        act.activation(hidT[:, j2], psH[j2].rearrange("p (j s) -> p j s", j=2), ACT.Copy)\
                            .then_inc(S["hidT"], 1)

                    def y_out(n, b, j2):
                        c = act.value_load(tab[0:1, 1, bass.ds(b, 1)], min_val=0, max_val=PAIRS)
                        act.wait_ge(S["down"], n)
                        act.wait_ge(S["ya"], n + 1)
                        act.activation(yT[:, 0:4, bass.ds(c, BLK)], psG[:, j2, 0, :].rearrange("p (n s) -> p n s", n=4),
                                       ACT.Copy).then_inc(S["ya"], 1)

                    act.wait_ge(S["tab"], 1)
                    T_out_upto(act, ("st", 1))
                    round_input(1, 1)
                    for k in range(2):
                        round_weights(k, 1, 1, 16)
                    tanh_gate(1, 0)

                    def act_block(i, d, ahead=2):
                        if ahead == 2:
                            with if_used(act, i, d + 2):
                                round_input(6 * i + (d + 2), d % 2)
                                round_weights(0, (d + 2) % 3, d % 2, arrived(i, d + 2))
                        with if_used(act, i, d):
                            hidden_out(6 * i + (d + 1), d % 2)
                        if ahead == 2:
                            with if_used(act, i, d + 2):
                                round_weights(1, (d + 2) % 3, d % 2, arrived(i, d + 2))
                        if ahead:
                            with if_used(act, i, d + 1):
                                tanh_gate(6 * i + (d + 2), (d + 1) % 2)
                        with if_used(act, i, d):
                            y_out(6 * i + (d + 1), 6 * i + d, d % 2)

                    load_extra(act)
                    with act.Fori(0, N_LOOP) as i:
                        for d in range(6):
                            act_block(i, d)
                    for d in range(N_TAIL):
                        act_block(N_LOOP, d, min(2, N_TAIL - 1 - d))
                    act.drain().then_inc(S["y_all"], 1)
                    for s in range(4):
                        T_out(("y", s, 0), yn[:, s, 0:512])

                @block.gpsimd
                def _(pool):
                    def twice(dst, name, done):
                        c = SRC[name][0]
                        pool.tensor_copy(dst.rearrange("p t (a d) -> p t a d", a=2),
                                         z[:, :, c:c + DH].unsqueeze(2).broadcast_to([P, NT, 2, DH])).then_inc(done, 1)

                    for i, name in enumerate(TWINS):
                        pool.wait_ge(S["rope"], {"ki": 1, "ksel": 3, "kwin": 3}.get(name, 5))
                        twice(twin[:, :, i, :], name, S["twin"])
                        if name == "ki":
                            pool.wait_ge(S["rope"], 2)
                            for j, name in enumerate(TWINS_CMP):
                                twice(twin_cmp[:, :, j, :], name, S["twin_cmp"])

                @block.vector
                def _(dve):
                    n_link = [0]

                    def link(ins):
                        n_link[0] += 1
                        ins.then_inc(S["dve"], 1)
                        dve.wait_ge(S["dve"], n_link[0])

                    TT, TS, STT = dve.tensor_tensor, dve.tensor_scalar, dve.scalar_tensor_tensor

                    dve.wait_ge(S["small"], 1)
                    g, done = G_ready(dve, "bc")
                    dve.tensor_copy(bc[:, :], g[:, 0, 0:80]).then_inc(done, 1)
                    dve.wait_ge(done, 1)
                    dve.wait_ge(S["ss"], NT)
                    TS(rms, ss, 1.0 / D, EPS, ALU.mult, ALU.add).then_inc(S["ms"], 1)
                    dve.wait_ge(S["rms"], 1)
                    link(dve.reciprocal(rstd, rms))
                    for t in range(NT):
                        TS(hn[:, t, :], h[:, t, :], rstd[:, t:t + 1], None, ALU.mult).then_inc(S["hn"], 1)

                    def hnT_out(kind, gain):
                        for t in range(NT):
                            for q in range(2):
                                bank, done = T_ready(dve, (kind, t, q))
                                TT(hnT[:, 4 * q:4 * q + 4, t * P:(t + 1) * P], bank.rearrange("p (k t) -> p k t", k=4),
                                   gain[:, 4 * q:4 * q + 4].unsqueeze(2).broadcast_to([P, 4, P]), ALU.mult
                                   ).then_inc(S["hnt"], 1)
                                fence(done)

                    n_h = [0]

                    def fence(done):
                        n_h[0] += 1
                        dve.wait_ge(S["hnt"], n_h[0])
                        dve.sem_inc(done, 1)

                    def rest_of_piece(q):
                        if q >= len(SPLIT):
                            return
                        i = PLACE[PIECE[SPLIT[q]]]
                        dve.wait_ge(S["ahi"], q + 1)
                        c = 4 * width(SPLIT[q])
                        TT(a_lo[i][:, 0:c], piece[i][:, 0:c], a_hi[q % NHI][:, 0:c].bitcast(F32), ALU.subtract)\
                            .then_inc(S["alo"], 1)

                    gate_at = [0]

                    def rest_of_item(i):
                        for half in range(2):
                            rest_of_piece(2 * i + half)

                    def gate_rest(n):
                        for _ in range(n):
                            if gate_at[0] < len(GATES):
                                i, t = GATES[gate_at[0]]
                                gate_at[0] += 1
                                if not t and i != 1:
                                    rest_of_item(NZ + i + 1)

                    hnT_out("hn", gain1)
                    for t in range(NT):
                        for q in range(2):
                            dve.wait_ge(S["nhi"], 2 * t + q + 1)
                            a = hnT[:, 4 * q:4 * q + 4, t * P:(t + 1) * P]
                            TT(hn_lo[:, 4 * q:4 * q + 4, t * P:(t + 1) * P], a,
                               hn_hi[:, 4 * q:4 * q + 4, t * P:(t + 1) * P].bitcast(F32), ALU.subtract).then_inc(S["nlo"], 1)
                    for q in range(2 * NZ + 2):
                        rest_of_piece(q)
                    G_out_upto(dve, ("z", WIN[-1]))
                    link(TT(fx, z[:, :, ZOFF["f_b"]:ZOFF["f_b"] + H],
                            bc[:, 72:76].unsqueeze(1).broadcast_to([P, NT, H]), ALU.add))
                    link(TS(fa, fx, -1.0, None, ALU.mult))
                    TT(fa, fa, fx, ALU.min).then_inc(S["foxneg"], 1)
                    dve.wait_ge(S["ckvss"], NT)
                    TS(crms, css, 1.0 / P, EPS, ALU.mult, ALU.add).then_inc(S["ckvms"], 1)

                    def rope(x, n, tmps):
                        c = cos[:, :, :].unsqueeze(2).broadcast_to([P, NT, n, DH])
                        s = sin[:, :, :].unsqueeze(2).broadcast_to([P, NT, n, DH])
                        a, b = (v[:, 0:NT * n * DH].rearrange("p (t n d) -> p t n d", t=NT, n=n) for v in tmps)
                        TT(a, x, c, ALU.mult)
                        TT(b[:, :, :, 0:32], x[:, :, :, 32:64], s[:, :, :, 0:32], ALU.mult)
                        link(TT(b[:, :, :, 32:64], x[:, :, :, 0:32], s[:, :, :, 32:64], ALU.mult))
                        return TT(x, a, b, ALU.add)

                    def rope_group(i):
                        c, n, step = ROPE[i]
                        x = z[:, :, c:c + n * step].rearrange("p t (n s) -> p t n s", s=step)[:, :, :, 0:DH] \
                            if step != DH else z[:, :, c:c + n * DH].rearrange("p t (n s) -> p t n s", s=DH)
                        m = rope(x, n, [oall[:, t].rearrange("p i w -> p (i w)") for t in range(NT)])
                        m.then_inc(S["rope"], 1)
                        n_rope[0] += 1
                        dve.wait_ge(S["rope"], n_rope[0])

                    n_rope = [0]
                    dve.wait_ge(S["hnt"], 4)
                    rope_group(3)
                    dve.wait_ge(S["foxln"], 2)
                    link(TS(fx, fx, 0.0, None, ALU.min))
                    TT(logf, fx, fa, ALU.subtract).then_inc(S["logf"], 1)
                    gate_rest(2)
                    rope_group(1)
                    link(TS(wi, z[:, :, ZOFF["w_i"]:ZOFF["w_i"] + H], 0.5, None, ALU.mult))
                    rope_group(0)
                    dve.wait_ge(S["ckvrms"], 1)
                    link(dve.reciprocal(crstd, crms))
                    for t in range(NT):
                        m = TS(kvs[:, t, 0:P], z[:, t, ZOFF["ckv"]:ZOFF["ckv"] + P], crstd[:, t:t + 1], None, ALU.mult)
                    m.then_inc(S["ckvn"], 1)
                    gate_rest(2)
                    rope_group(2)
                    rope_group(4)
                    link(TS(ga, ga, 0.5, 0.5, ALU.mult, ALU.add))
                    T_out_upto(dve, ("src", 4))
                    for odd in range(2):
                        p = slice(DH * odd, DH * odd + DH)
                        for a in range(2):
                            first = TSLOT["kcmp"]
                            m = TT(zc[p, :, 8 * a:8 * a + 8, :],
                                   tr[p, first:first + 2, 16 * a:16 * a + 16 * N_CMP].rearrange(
                                       "p j (w c b) -> p b j c w", c=8, b=2)[:, odd],
                                   peT[p, :].rearrange("p (j c) -> p j c", j=2)[:, :, 8 * a:8 * a + 8].unsqueeze(3)
                                   .broadcast_to([DH, 2, 8, N_CMP]), ALU.add)
                    m.then_inc(S["zc"], 1)
                    for t in range(NT):
                        w = P * (t + 1)
                        i = G_AT[("idx", t)]
                        dve.wait_ge(S[f"ge{i % 2}"], i // 2 + 1)
                        link(TS(sel[:, t, 0:w], sm[t][:, AT[0], 0:w], wi[:, t, 0:1], None, ALU.mult))
                        for x in range(1, H):
                            link(STT(out=sel[:, t, 0:w], in0=sm[t][:, AT[x], 0:w], scalar=wi[:, t, x:x + 1],
                                     in1=sel[:, t, 0:w], op0=ALU.mult, op1=ALU.add))
                        link(TT(sel[:, t, 0:w], sel[:, t, 0:w], causal[t], ALU.add))
                    i = G_AT["kvc"]
                    dve.wait_ge(S[f"ge{i % 2}"], i // 2 + 1)
                    m = rope(kvs[:, :, 0:W].rearrange("p t (n s) -> p t n s", s=DH), H,
                             [ptb[:, 0:512], ptb[:, 512:1024]])
                    m.then_inc(S["kvrope"], 1)
                    rest_of_item(NZ + 2)
                    i = G_AT["cmph"]
                    dve.wait_ge(S[f"ge{i % 2}"], i // 2 + 1)
                    link(TS(gb, gb, 0.044715, 1.0, ALU.mult, ALU.add))
                    TT(gb, gb, gx, ALU.mult).then_inc(S["gelu_b"], 1)
                    dve.wait_ge(S["gelu_th"], 1)
                    STT(out=gx, in0=gb, scalar=1.0, in1=gx, op0=ALU.add, op1=ALU.mult).then_inc(S["gelu"], 1)

                    def topk(t, half):
                        w = P * (t + 1)
                        a = sel[:, t, 0:w]
                        for _ in range(TOPK // 16):
                            link(dve.max(m8, a))
                            link(dve.match_replace(a, m8, a, TAKEN))
                        if not half:
                            return
                        link(TS(a, a, TAKEN, -1.0, ALU.is_equal, ALU.add))
                        link(STT(out=a, in0=a, scalar=-NEG, in1=causal[t], op0=ALU.mult, op1=ALU.add))

                    sinks = bc[:, 76:80].rearrange("p (b a) -> p b a", b=2)

                    def softmax_in(u):
                        m_, t = UNITS[u]
                        w = N_CMP if m_ == "cmp" else P * (t + 1)
                        mask = {"cmp": cmp_mask, "swa": swa_mask, "dsa": [sel[:, i, 0:P * (i + 1)] for i in range(NT)]
                                }.get(m_, causal)[t]
                        g, done = G_ready(dve, ("s", u))
                        if u >= 2:
                            dve.wait_ge(S["pv"], u - 1)
                        s = sm[u % 2][:, :, 0:w]
                        STT(out=s, in0=g.rearrange("p a (b s) -> p (a b) s", b=2)[:, :, 0:w], scalar=SCALE,
                            in1=mask.unsqueeze(1).broadcast_to([P, H, w]), op0=ALU.mult, op1=ALU.add).then_inc(done, 1)
                        i = G_AT[("s", u)]
                        dve.wait_ge(done, i // 2 + 1)
                        if m_ == "swa":
                            link(dve.reduce_max(nmx[:, u, :], s, AXX))
                            link(TT(by_head(nmx[:, u, :]), by_head(nmx[:, u, :]), sinks, ALU.max))
                            link(TS(nmx[:, u, :], nmx[:, u, :], -1.0, None, ALU.mult))
                            TT(by_head(nmx[:, 12 + t, :]), by_head(nmx[:, u, :]), sinks, ALU.add).then_inc(S["sink"], 1)
                            dve.wait_ge(S["sink"], t + 1)
                            dve.sem_inc(S["sm"], 1)
                        else:
                            dve.reduce_max(nmx[:, u, :], s, AXX, negate=True).then_inc(S["sm"], 1)

                    def combine(u):
                        m_, t = UNITS[u]
                        dve.wait_ge(S["exp"], H * (u + 1))
                        if m_ == "swa":
                            dve.wait_ge(S["sinkexp"], t + 1)
                            link(TT(ssum[:, u, :], ssum[:, u, :], ssum[:, 12 + t, :], ALU.add))
                        link(dve.reciprocal(coef, ssum[:, u, :]))
                        if m_ in GATE_OF:
                            link(TT(by_head(coef), by_head(coef),
                                    ga[:, t, :, GATE_OF[m_]].rearrange("p (b a) -> p b a", b=2), ALU.mult))
                        if m_ == "cmp":
                            link(TS(coef, coef, C("cmp_row")[:, t:t + 1], None, ALU.mult))
                        dve.wait_ge(S["pv"], u + 1)
                        o = oall[:, t, OUT_OF[m_], :].rearrange("p (h d) -> p h d", h=H)
                        add = m_ in ("win", "cmp")
                        dst = otmp[:, :].rearrange("p (h d) -> p h d", h=H) if add else o
                        m = TT(dst.rearrange("p (b a) d -> p b a d", b=2),
                               psO[:, u % 2, :].rearrange("p (b a d) -> p b a d", b=2, a=2),
                               by_head(coef).unsqueeze(3).broadcast_to([P, 2, 2, DH]), ALU.mult)
                        if add:
                            link(m)
                            m = TT(o, o, dst, ALU.add)
                        m.then_inc(S["oc"], 1)
                        dve.wait_ge(S["oc"], u + 1)

                    NU = len(UNITS)
                    softmax_in(0)
                    gate_rest(2)
                    for u in range(NU):
                        if u + 1 < NU:
                            softmax_in(u + 1)
                        combine(u)
                        if u in (1, 3, 5, 7):
                            topk(u // 4, u // 2 % 2)
                        gate_rest(1)
                    dve.wait_ge(S["gate_out"], len(GATES))
                    for t in range(NT):
                        for n in range(2):
                            for i2 in range(2):
                                g, done = G_ready(dve, ("mg", t, n, i2))
                                o = merged[:, t, 512 * n:512 * n + 512]
                                for j in range(2):
                                    first = not i2 and not j
                                    m = STT(out=o if first else mtmp, in0=gt[:, t, 2 * i2 + j, 512 * n:512 * n + 512],
                                            scalar=1.0, in1=g[:, j, :], op0=ALU.add, op1=ALU.mult)
                                    link(m)
                                    if not first:
                                        m = TT(o, o, mtmp, ALU.add)
                                        if j:
                                            m.then_inc(done, 1)
                                            dve.wait_ge(done, G_AT[("mg", t, n, i2)] // 2 + 1)
                                        else:
                                            link(m)
                    for t in range(NT):
                        g, done = G_ready(dve, ("wo", t))
                        TT(h[:, t, :], h[:, t, :], g.rearrange("p a n -> p (a n)"), ALU.add).then_inc(done, 1)
                        dve.wait_ge(done, G_AT[("wo", t)] // 2 + 1)
                        dve.sem_inc(S["h"], 1)
                        dve.wait_ge(S["ss2"], t + 1)
                        TS(rms[:, t:t + 1], ss[:, t:t + 1], 1.0 / D, EPS, ALU.mult, ALU.add).then_inc(S["ms2"], 1)
                        dve.wait_ge(S["rms2"], t + 1)
                        link(dve.reciprocal(rstd[:, t:t + 1], rms[:, t:t + 1]))
                        TS(hn[:, t, :], h[:, t, :], rstd[:, t:t + 1], None, ALU.mult).then_inc(S["hn2"], 1)
                    dve.memset(xs[:, :, PAIRS:SLOTS], 0.0).then_inc(S["pad"], 1)
                    dve.wait_ge(S["small2"], 16 * 8)
                    hnT_out("hn2", gain2)
                    for t in range(NT):
                        dve.wait_ge(S["gather_hi"], t + 1)
                        TT(gather_lo[:, t, :], hn[:, t, :], gather_hi[:, t, :].bitcast(F32), ALU.subtract)\
                            .then_inc(S["gather_lo"], 1)

                    g, done = G_ready(dve, "router")
                    dve.tensor_copy(lg, g[:, :, 0:GROUPS + E]).then_inc(done, 1)
                    dve.wait_ge(done, G_AT["router"] // 2 + 1)
                    gl, el = lg[:, :, 0:GROUPS], lg[:, :, GROUPS:]

                    def first_max(x, n, v, oh_, tmp, rank):
                        link(dve.reduce_max(v, x, AXX))
                        link(TT(tmp, x, v.unsqueeze(2).broadcast_to([P, NT, n]), ALU.is_equal))
                        link(TT(tmp, tmp, rank.unsqueeze(1).broadcast_to([P, NT, n]), ALU.mult))
                        link(dve.reduce_max(ee, tmp, AXX))
                        link(TT(oh_, tmp, ee.unsqueeze(2).broadcast_to([P, NT, n]), ALU.is_equal))

                    first_max(gl, GROUPS, gmx, ohg, g8, C("rank8"))
                    TT(g8b, gl, gmx.unsqueeze(2).broadcast_to([P, NT, GROUPS]), ALU.subtract).then_inc(S["gexp_in"], 1)
                    link(TS(g8, ohg, 1.0, -NEG, ALU.subtract, ALU.mult))
                    link(TT(em.rearrange("p t (g e) -> p t g e", g=GROUPS), el.rearrange("p t (g e) -> p t g e", g=GROUPS),
                            g8.unsqueeze(3).broadcast_to([P, NT, GROUPS, PER_GROUP]), ALU.add))
                    first_max(em, E, v1, oh1, eq, C("rank64"))
                    link(STT(out=em, in0=oh1, scalar=NEG, in1=em, op0=ALU.mult, op1=ALU.add))
                    first_max(em, E, v2, oh2, eq, C("rank64"))
                    TT(oh, oh1, oh2, ALU.add).then_inc(S["oh"], 1)
                    TT(ee, v2, v1, ALU.subtract).then_inc(S["texp_in"], 1)
                    dve.wait_ge(S["gexp"], 1)
                    link(dve.reduce_sum(pg, g8b, AXX))
                    link(dve.reciprocal(pg, pg))
                    g, done = G_ready(dve, "tot")
                    link(dve.tensor_copy(cnt[0:E, 0:1], g[0:E, 0, 0:1]))
                    link(TS(cnt[0:E, 1:2], cnt[0:E, 0:1], 0.5, None, ALU.is_gt))
                    link(STT(out=cnt[0:E, 1:2], in0=cnt[0:E, 0:1], scalar=BLK + 0.5, in1=cnt[0:E, 1:2],
                             op0=ALU.is_gt, op1=ALU.add))
                    TS(totbc, ones[0:E, :], cnt[0:E, 0:1], None, ALU.mult).then_inc(done, 1)
                    dve.wait_ge(done, G_AT["tot"] // 2 + 1)
                    dve.sem_inc(S["cnt"], 1)
                    dve.wait_ge(S["texp"], 1)
                    link(TS(w1s, ee, 1.0, None, ALU.add))
                    link(dve.reciprocal(w1s, w1s))
                    link(TT(w1s, w1s, pg, ALU.mult))
                    link(TT(w2s, w1s, ee, ALU.mult))
                    g, done = G_ready(dve, "pos")
                    link(dve.tensor_copy(pos[0:E, :], g[0:E, 0, 0:2]))
                    place = g[:, 1, 0:NT * E].rearrange("p (t e) -> p t e", t=NT)
                    link(TT(eq, oh1, place, ALU.mult))
                    link(dve.reduce_sum(d1, eq, AXX))
                    link(TT(eq, oh2, place, ALU.mult))
                    dve.reduce_sum(d2, eq, AXX).then_inc(done, 1)
                    dve.wait_ge(done, G_AT["pos"] // 2 + 1)
                    blkn = C("block")[0:E, :]
                    link(TT(bend[0:E], pos[0:E, 1:2], cnt[0:E, 1:2], ALU.add))
                    link(TS(c0[0:E], pos[0:E, 1:2], -float(BLK), None, ALU.mult))
                    link(TT(c0[0:E], c0[0:E], pos[0:E, 0:1], ALU.add))
                    link(TS(blk3[:, 1, :], blkn, pos[0:E, 1:2], None, ALU.is_ge))
                    link(STT(out=blk3[:, 2, :], in0=blkn, scalar=bend[0:E], in1=blk3[:, 1, :], op0=ALU.is_lt,
                             op1=ALU.mult))
                    link(TS(blk3[:, 0, :], blkn, float(BLK), c0[0:E], ALU.mult, ALU.add))
                    link(TT(blk3[:, 0, :], blk3[:, 0, :], blk3[:, 2, :], ALU.mult))
                    TS(blk3[:, 1, :], blk3[:, 2, :], C("expert")[0:E], None, ALU.mult).then_inc(S["blk3"], 1)
                    slots = C("slot")
                    for t in range(NT):
                        link(TS(onehot[:, t, :], slots, d1[:, t:t + 1], None, ALU.is_equal))
                        link(STT(out=onehot[:, t, :], in0=slots, scalar=d2[:, t:t + 1], in1=onehot[:, t, :].bitcast(F32),
                                 op0=ALU.is_equal, op1=ALU.add))
                    dve.sem_inc(S["p01"], 1)
                    g, done = G_ready(dve, "blk")
                    b3 = g[0:1, 0, 0:3 * NBLK].rearrange("p (a b) -> p a b", a=3)
                    link(TS(tabf[:, 0, :], b3[:, 2, :], -1.0, 1.0, ALU.mult, ALU.add))
                    link(STT(out=tab[:, 1, :], in0=tabf[:, 0, :], scalar=float(PAIRS), in1=b3[:, 0, :],
                             op0=ALU.mult, op1=ALU.add))
                    STT(out=tab[:, 0, :], in0=tabf[:, 0, :], scalar=float(E - 1), in1=b3[:, 1, :],
                        op0=ALU.mult, op1=ALU.add).then_inc(done, 1)
                    dve.wait_ge(done, G_AT["blk"] // 2 + 1)
                    dve.sem_inc(S["tab"], 1)
                    for t in range(NT):
                        link(TS(weighted[:, t, :], slots, d1[:, t:t + 1], w1s[:, t:t + 1], ALU.is_equal, ALU.mult))
                        link(TS(mtmp, slots, d2[:, t:t + 1], w2s[:, t:t + 1], ALU.is_equal, ALU.mult))
                        link(TT(weighted[:, t, :], weighted[:, t, :], mtmp, ALU.add))
                    dve.sem_inc(S["pw"], 1)
                    for i in (1, 3):
                        g, done = G_ready(dve, ("ga", i))
                        for j in range(2):
                            m = TS(xs[:, 2 * i + j, 0:PAIRS], g[:, j, :], gain2[:, 2 * i + j:2 * i + j + 1], None, ALU.mult)
                        m.then_inc(done, 1)
                    for i in range(2):
                        bank, done = T_ready(dve, ("st", i))
                        dve.tensor_copy(stt_[:, 2 * i:2 * i + 2, :].rearrange("p s t -> p (s t)"), bank).then_inc(done, 1)

                    def rest_of_block(b, n, j3, j2):
                        c = dve.value_load(tab[0:1, 1, bass.ds(b, 1)], min_val=0, max_val=PAIRS)
                        dve.wait_ge(S["xh"], n)
                        TT(x_lo[j2][:, :, :], xs[:, :, bass.ds(c, BLK)], x_hi[j2][:, :, :].bitcast(F32), ALU.subtract)\
                            .then_inc(S["xl"], 1)
                        for k in range(2):
                            dve.wait_ge(S["whi"], 2 * n + (k - 1))
                            w = eslot[j3][:, 2048 * k:2048 * (k + 1)].rearrange("p (k n) -> p k n", k=KC)
                            TT(w_lo[j3][:, k], w, w_hi[j2][:, k].bitcast(F32), ALU.subtract).then_inc(S["wlo"], 1)

                    def swiglu(n, j2):
                        dve.wait_ge(S["th"], n)
                        STT(out=hida[:, j2], in0=th[:, j2], scalar=1.0, in1=psT[:, j2, 0:DE], op0=ALU.add, op1=ALU.mult)\
                            .then_inc(S["hid_a"], 1)
                        dve.wait_ge(S["hid_a"], n)
                        STT(out=hid[:, j2], in0=hida[:, j2], scalar=0.5, in1=psT[:, j2, DE:2 * DE], op0=ALU.mult,
                            op1=ALU.mult).then_inc(S["hid"], 1)

                    def y_out(n, b, j2):
                        c = dve.value_load(tab[0:1, 1, bass.ds(b, 1)], min_val=0, max_val=PAIRS)
                        dve.wait_ge(S["down"], n)
                        dve.wait_ge(S["yd"], n + 1)
                        dve.tensor_copy(yT[:, 4:8, bass.ds(c, BLK)], psG[:, j2, 1, :].rearrange("p (n s) -> p n s", n=4))\
                            .then_inc(S["yd"], 1)

                    def dve_block(i, d, ahead=2):
                        if ahead == 2:
                            with if_used(dve, i, d + 2):
                                rest_of_block(6 * i + (d + 2), 6 * i + (d + 3), (d + 2) % 3, d % 2)
                        if ahead:
                            with if_used(dve, i, d + 1):
                                swiglu(6 * i + (d + 2), (d + 1) % 2)
                        with if_used(dve, i, d):
                            y_out(6 * i + (d + 1), 6 * i + d, d % 2)

                    rest_of_block(0, 1, 0, 0)
                    rest_of_block(1, 2, 1, 1)
                    swiglu(1, 0)
                    load_extra(dve)
                    with dve.Fori(0, N_LOOP) as i:
                        for d in range(6):
                            dve_block(i, d)
                    for d in range(N_TAIL):
                        dve_block(N_LOOP, d, min(2, N_TAIL - 1 - d))
                    dve.drain().then_inc(S["y_all"], 1)
                    for s in range(4):
                        bank, done = T_ready(dve, ("y", s, 1))
                        dve.tensor_copy(yn[:, s, 512:1024], bank).then_inc(done, 1)
                    for t in range(NT):
                        g, done = G_ready(dve, ("sc", t))
                        link(TT(h[:, t, :], h[:, t, :], g.rearrange("p a n -> p (a n)"), ALU.add))

            nc.all_engine_barrier()
            engines = (nc.sync, nc.scalar, nc.vector, nc.tensor, nc.gpsimd)
            for i, n in enumerate(ALL_SEMS):
                engines[i % len(engines)].sem_clear(S[n])
            nc.all_engine_barrier()

        with nc.Block() as block:
            @block.tensor
            def _(pe):
                pe.wait_ge(s_pre["dma"], 80)
                for n in range(2):
                    m = pe.matmul(psG[:, 0, n, :], ones[0:1, :], fin[0:1, 512 * n:512 * n + 512], start=True, stop=True)
                m.then_inc(s_pre["g"], 1)

            @block.scalar
            def _(act):
                for t in range(NT):
                    act.activation(hn[:, t, :], h[:, t, :], ACT.Square, accum_out=ss[:, t:t + 1]).then_inc(s_pre["ss"], 1)
                act.wait_ge(s_pre["ms"], 1)
                act.activation(rms, rms, ACT.Sqrt).then_inc(s_pre["rms"], 1)

            @block.vector
            def _(dve):
                dve.wait_ge(s_pre["ss"], NT)
                dve.tensor_scalar(rms, ss, 1.0 / D, EPS, ALU.mult, ALU.add).then_inc(s_pre["ms"], 1)
                dve.wait_ge(s_pre["rms"], 1)
                dve.reciprocal(rstd, rms).then_inc(s_pre["fin"], 1)
                dve.wait_ge(s_pre["fin"], 1)
                dve.wait_ge(s_pre["g"], 1)
                for t in range(NT):
                    dve.scalar_tensor_tensor(out=hn[:, t, :], in0=h[:, t, :], scalar=rstd[:, t:t + 1],
                                             in1=psG[:, 0].rearrange("p a n -> p (a n)"), op0=ALU.mult, op1=ALU.mult
                                             ).then_inc(s_pre["y"], 1)

            @block.sync
            def _(sp):
                sp.dma_start(fin, A["final_norm"].rearrange("(a d) -> a d", a=1)).then_inc(s_pre["dma"], 16)
                for t in range(NT):
                    sp.wait_ge(s_pre["y"], t + 1)
                    sp.dma_start(out[0, t * P:(t + 1) * P, :], hn[:, t, :]).then_inc(s_pre["out"], 16)
                sp.wait_ge(s_pre["out"], 16 * NT)


_INS = ["x", "positions", "attn_norm", "w_in", "nsa_pe_k", "nsa_w1_k", "nsa_w2_k", "nsa_pe_v", "nsa_w1_v", "nsa_w2_v",
        "fox_forget_bias", "dsa_kv_norm", "dsa_w_ukv", "swa_sinks", "w_branch", "w_gate", "w_out", "ffn_norm",
        "moe_w_group", "moe_b_group", "moe_w_expert", "moe_b_expert", "moe_w_gate", "moe_w_up", "moe_w_down",
        "final_norm"]


def kernel(**inputs):
    import concourse.bacc as _bacc
    from concourse.bass_utils import run_bass_kernel_spmd as _run

    nc = _bacc.Bacc("TRN2", target_bir_lowering=False, num_devices=1)
    arrays = {name: np.ascontiguousarray(inputs[name]) for name in _INS}
    arrays["consts"] = constants()
    args = {name: nc.dram_tensor(f"in_{name}", a.shape, mybir.dt.from_np(a.dtype), kind="ExternalInput").ap()
            for name, a in arrays.items()}
    out = nc.dram_tensor("out_0", (1, T, D), F32, kind="ExternalOutput").ap()
    trunk(nc, args, out)
    r = _run(nc, [{f"in_{name}": a for name, a in arrays.items()}], core_ids=[0])
    return r.results[0]["out_0"]
```
